# Optimizing a Trainium2 kernel written in Bass

```python
import jax, jax.numpy as jnp
from jax import lax
import numpy as np
import math
import jax
import jax.numpy as jnp

D_MODEL = 1024
BATCH = 1
SEQ = 256
DEPTH = 2

GRID_W = 64
CTX_LEN = 256
HEAD_DIM = 64
ATTN_SCALE = HEAD_DIM ** -0.5
CONV_A_CH = D_MODEL // 2
CONV_A_WIDTH = 31
CONV_B_CH = D_MODEL // 2
CONV_B_WIDTH = 3
CONV_SPLITS = [CONV_A_CH, 2 * CONV_A_CH, 2 * CONV_A_CH + CONV_B_CH, 2 * CONV_A_CH + 2 * CONV_B_CH]
CONV_IN_COLS = 2 * CONV_A_CH + 3 * CONV_B_CH
CONV_OUT_ROWS = CONV_A_CH + CONV_B_CH
GQA_Q_HEADS = (D_MODEL // 2) // HEAD_DIM
GQA_KV_HEADS = GQA_Q_HEADS // 4
NA_HEADS = (D_MODEL // 2) // HEAD_DIM
NA_WIN_ROWS = 8
NA_WIN_COLS = 16
Q_BLOCK = 128
ROPE_THETA = 10000.0
ROPE_AXIS_DIM = HEAD_DIM // 2
Q_COLS_C = GQA_Q_HEADS * HEAD_DIM
KV_COLS_C = GQA_KV_HEADS * HEAD_DIM
COLS_D = NA_HEADS * HEAD_DIM
ATTN_SPLITS = [Q_COLS_C, Q_COLS_C + KV_COLS_C, Q_COLS_C + 2 * KV_COLS_C,
               Q_COLS_C + 2 * KV_COLS_C + COLS_D, Q_COLS_C + 2 * KV_COLS_C + 2 * COLS_D]
ATTN_IN_COLS = Q_COLS_C + 2 * KV_COLS_C + 3 * COLS_D
ATTN_OUT_ROWS = Q_COLS_C + COLS_D
N_GROUPS = 4
EXPERTS_PER_GROUP = 8
N_EXPERTS = N_GROUPS * EXPERTS_PER_GROUP
TOP_K_INNER = 2
EXPERT_HIDDEN = D_MODEL // 2
DISPATCH_BLOCK = 128
DEEPNORM_ALPHA = (2 * DEPTH) ** 0.25
DEEPNORM_BETA = (8 * DEPTH) ** -0.25
N_EVEN = (DEPTH + 1) // 2
N_ODD = DEPTH // 2
LN_EPS = 1e-5
RMS_EPS = 1e-6


def layer_norm(x, g, b):
    xf = x.astype(jnp.float32)
    mu = jnp.mean(xf, axis=-1, keepdims=True)
    var = jnp.mean(jnp.square(xf - mu), axis=-1, keepdims=True)
    return ((xf - mu) * lax.rsqrt(var + LN_EPS) * g + b).astype(x.dtype)

def rms_norm(x, g):
    xf = x.astype(jnp.float32)
    return (xf * lax.rsqrt(jnp.mean(xf * xf, axis=-1, keepdims=True) + RMS_EPS) * g).astype(x.dtype)

def ada_split(cond, w, b):
    return jnp.split(jax.nn.silu(cond) @ w + b, 6, axis=-1)

def depthwise_conv(h, w):
    k = w.shape[0]
    return lax.conv_general_dilated(h, w[:, None, :].astype(h.dtype), (1,), [(k // 2, k // 2)],
                                    dimension_numbers=('NWC', 'WIO', 'NWC'),
                                    feature_group_count=h.shape[-1])

def split_heads(z, n):
    b, l, _ = z.shape
    return z.reshape(b, l, n, HEAD_DIM).transpose(0, 2, 1, 3)

def merge_heads(o):
    b, n, l, d = o.shape
    return o.transpose(0, 2, 1, 3).reshape(b, l, n * d)

def axial_rope_tables(n_tokens):
    t = jnp.arange(n_tokens)
    row = (t // GRID_W).astype(jnp.float32)
    col = (t % GRID_W).astype(jnp.float32)
    inv = ROPE_THETA ** (-jnp.arange(0, ROPE_AXIS_DIM, 2, dtype=jnp.float32) / ROPE_AXIS_DIM)
    ar = row[:, None] * inv
    ac = col[:, None] * inv
    return jnp.cos(ar), jnp.sin(ar), jnp.cos(ac), jnp.sin(ac)

def rotate(x, cos, sin):
    x1, x2 = jnp.split(x, 2, axis=-1)
    return jnp.concatenate([x1 * cos - x2 * sin, x1 * sin + x2 * cos], axis=-1)

def apply_axial_rope(x, tables):
    cr, sr, cc, sc = [t.astype(x.dtype) for t in tables]
    xr, xc = jnp.split(x, 2, axis=-1)
    return jnp.concatenate([rotate(xr, cr, sr), rotate(xc, cc, sc)], axis=-1)

def softmax_attention(q, k, v):
    s = jnp.einsum('bkgqd,bksd->bkgqs', q, k, preferred_element_type=jnp.float32) * ATTN_SCALE
    p = jax.nn.softmax(s, axis=-1).astype(v.dtype)
    return jnp.einsum('bkgqs,bksd->bkgqd', p, v)

def gqa_latent(q, k_all, v_all):
    b, hk, g, s, d = q.shape
    nb = s // Q_BLOCK
    qb = jnp.moveaxis(q.reshape(b, hk, g, nb, Q_BLOCK, d), 3, 0)
    o = lax.map(lambda qi: softmax_attention(qi, k_all, v_all), qb)
    return jnp.moveaxis(o, 0, 3).reshape(b, hk * g, s, d)

def neighbourhood_latent(q, k, v, k_ctx, v_ctx, rel_bias):
    b, h, s, d = q.shape
    rows = s // GRID_W
    kr = min(NA_WIN_ROWS, rows)
    n_ctx = k_ctx.shape[2]
    qg = jnp.moveaxis(q.reshape(b, h, rows, GRID_W, d), 2, 0)
    kg = k.reshape(b, h, rows, GRID_W, d)
    vg = v.reshape(b, h, rows, GRID_W, d)
    qcol = jnp.arange(GRID_W)
    cstart = jnp.clip(qcol - NA_WIN_COLS // 2, 0, GRID_W - NA_WIN_COLS)
    in_win = (qcol[None, :] >= cstart[:, None]) & (qcol[None, :] < cstart[:, None] + NA_WIN_COLS)
    col_idx = jnp.clip(qcol[None, :] - qcol[:, None] + NA_WIN_COLS - 1, 0, 2 * NA_WIN_COLS - 2)
    bias_cols = rel_bias[:, :, col_idx]

    def one_row(args):
        qr, r = args
        rs = jnp.clip(r - kr // 2, 0, rows - kr)
        kb = lax.dynamic_slice_in_dim(kg, rs, kr, axis=2)
        vb = lax.dynamic_slice_in_dim(vg, rs, kr, axis=2)
        s_lat = jnp.einsum('bhqd,bhrkd->bhqrk', qr, kb, preferred_element_type=jnp.float32) * ATTN_SCALE
        row_idx = rs + jnp.arange(kr) - r + NA_WIN_ROWS - 1
        bias = jnp.take(bias_cols, row_idx, axis=1).transpose(0, 2, 1, 3).astype(jnp.float32)
        s_lat = jnp.where(in_win[:, None, :], s_lat + bias, -jnp.inf).reshape(b, h, GRID_W, kr * GRID_W)
        s_ctx = jnp.einsum('bhqd,bhcd->bhqc', qr, k_ctx, preferred_element_type=jnp.float32) * ATTN_SCALE
        p = jax.nn.softmax(jnp.concatenate([s_ctx, s_lat], axis=-1), axis=-1).astype(v.dtype)
        p_ctx = p[..., :n_ctx]
        p_lat = p[..., n_ctx:].reshape(b, h, GRID_W, kr, GRID_W)
        return (jnp.einsum('bhqc,bhcd->bhqd', p_ctx, v_ctx)
                + jnp.einsum('bhqrk,bhrkd->bhqd', p_lat, vb))

    o = lax.map(one_row, (qg, jnp.arange(rows)))
    return jnp.moveaxis(o, 0, 2).reshape(b, h, s, d)

def conv_mixers(h, w_in, w_out, a_dw_w, a_dw_b, a_ln_g, a_ln_b, b_dw_w):
    z = h @ w_in
    a_val, a_gate, b_gate, c_gate, b_val = jnp.split(z, CONV_SPLITS, axis=-1)
    ya = a_val * jax.nn.sigmoid(a_gate)
    ya = depthwise_conv(ya, a_dw_w) + a_dw_b
    ya = jax.nn.silu(layer_norm(ya, a_ln_g, a_ln_b))
    yb = b_gate * depthwise_conv(c_gate * b_val, b_dw_w)
    return jnp.concatenate([ya, yb], axis=-1) @ w_out

def attn_mixers(h_lat, h_ctx, w_in, w_out, q_g, k_g, rel_bias, with_ctx_out):
    b, s, _ = h_lat.shape
    n_ctx = h_ctx.shape[1]
    group = GQA_Q_HEADS // GQA_KV_HEADS
    ql_c, kl_c, vl_c, ql_d, kl_d, vl_d = jnp.split(h_lat @ w_in, ATTN_SPLITS, axis=-1)
    qc_c, kc_c, vc_c, qc_d, kc_d, vc_d = jnp.split(h_ctx @ w_in, ATTN_SPLITS, axis=-1)
    tables = axial_rope_tables(s)
    q_lat = apply_axial_rope(rms_norm(split_heads(ql_c, GQA_Q_HEADS), q_g), tables)
    q_lat = q_lat.reshape(b, GQA_KV_HEADS, group, s, HEAD_DIM)
    k_lat = apply_axial_rope(rms_norm(split_heads(kl_c, GQA_KV_HEADS), k_g), tables)
    v_lat = split_heads(vl_c, GQA_KV_HEADS)
    k_ctx = rms_norm(split_heads(kc_c, GQA_KV_HEADS), k_g)
    v_ctx = split_heads(vc_c, GQA_KV_HEADS)
    o_c = gqa_latent(q_lat, jnp.concatenate([k_ctx, k_lat], axis=2), jnp.concatenate([v_ctx, v_lat], axis=2))
    kd_ctx = split_heads(kc_d, NA_HEADS)
    vd_ctx = split_heads(vc_d, NA_HEADS)
    o_d = neighbourhood_latent(split_heads(ql_d, NA_HEADS), split_heads(kl_d, NA_HEADS),
                               split_heads(vl_d, NA_HEADS), kd_ctx, vd_ctx, rel_bias)
    y_lat = jnp.concatenate([merge_heads(o_c), merge_heads(o_d)], axis=-1) @ w_out
    if not with_ctx_out:
        return y_lat, None
    q_ctx = rms_norm(split_heads(qc_c, GQA_Q_HEADS), q_g).reshape(b, GQA_KV_HEADS, group, n_ctx, HEAD_DIM)
    oc_c = softmax_attention(q_ctx, k_ctx, v_ctx).reshape(b, GQA_Q_HEADS, n_ctx, HEAD_DIM)
    oc_d = softmax_attention(split_heads(qc_d, NA_HEADS)[:, :, None], kd_ctx, vd_ctx)[:, :, 0]
    y_ctx = jnp.concatenate([merge_heads(oc_c), merge_heads(oc_d)], axis=-1) @ w_out
    return y_lat, y_ctx

def grouped_experts(x, expert, gate, w_gate, w_up, w_down):
    n, d = x.shape
    k = expert.shape[1]
    m = n * k
    flat_e = expert.reshape(m)
    flat_tok = jnp.arange(m) // k
    flat_w = gate.reshape(m)
    order = jnp.argsort(flat_e)
    se = flat_e[order]
    counts = jnp.bincount(flat_e, length=N_EXPERTS)
    padded = (counts + DISPATCH_BLOCK - 1) // DISPATCH_BLOCK * DISPATCH_BLOCK
    pad_end = jnp.cumsum(padded)
    pad_start = pad_end - padded
    start = jnp.cumsum(counts) - counts
    dest = pad_start[se] + jnp.arange(m) - start[se]
    n_blocks = -(-m // DISPATCH_BLOCK) + N_EXPERTS
    cap = n_blocks * DISPATCH_BLOCK
    slot_tok = jnp.full((cap,), n, jnp.int32).at[dest].set(flat_tok[order])
    slot_w = jnp.zeros((cap,), x.dtype).at[dest].set(flat_w[order])
    xs = jnp.concatenate([x, jnp.zeros((1, d), x.dtype)], axis=0)[slot_tok].reshape(n_blocks, DISPATCH_BLOCK, d)
    block_e = jnp.minimum(jnp.searchsorted(pad_end, jnp.arange(n_blocks) * DISPATCH_BLOCK, side='right'),
                          N_EXPERTS - 1)

    def run(args):
        xb, e = args
        return (jax.nn.silu(xb @ w_gate[e]) * (xb @ w_up[e])) @ w_down[e]

    ys = lax.map(run, (xs, block_e)).reshape(cap, d)
    return jnp.zeros((n + 1, d), x.dtype).at[slot_tok].add(ys * slot_w[:, None])[:n]

def hier_moe(tokens, w1, b1, w2, b2, w_gate, w_up, w_down):
    n = tokens.shape[0]
    p1 = jax.nn.softmax((tokens @ w1 + b1).astype(jnp.float32), axis=-1)
    p_grp, grp = lax.top_k(p1, 1)
    lg2 = (tokens @ w2 + b2).astype(jnp.float32).reshape(n, N_GROUPS, EXPERTS_PER_GROUP)
    lg2 = jnp.take_along_axis(lg2, grp[:, :, None], axis=1)[:, 0]
    top_val, top_idx = lax.top_k(lg2, TOP_K_INNER)
    gate = p_grp * jax.nn.softmax(top_val, axis=-1)
    expert = grp * EXPERTS_PER_GROUP + top_idx
    return grouped_experts(tokens, expert, gate.astype(tokens.dtype), w_gate, w_up, w_down)

def first_inputs(seed: int = 0) -> dict:
    key = jax.random.key(seed)
    keys = jax.random.split(key, 32)
    counter = [0]
    D = D_MODEL

    def nrm(shape, scale):
        kk = keys[counter[0]]
        counter[0] += 1
        return jax.random.normal(kk, shape, jnp.float32) * scale

    return {
        'x': nrm((BATCH, SEQ, D), 1.0),
        'c': nrm((BATCH, D), 1.0),
        'ctx': nrm((BATCH, CTX_LEN, D), 1.0),
        'c_ctx': nrm((D,), 1.0),
        'ada_w': nrm((DEPTH, D, 6 * D), 0.5 * D ** -0.5),
        'ada_b': nrm((DEPTH, 6 * D), 0.02),
        'ln1_g': 1.0 + nrm((DEPTH, D), 0.02),
        'ln1_b': nrm((DEPTH, D), 0.02),
        'ln2_g': 1.0 + nrm((DEPTH, D), 0.02),
        'ln2_b': nrm((DEPTH, D), 0.02),
        'conv_w_in': nrm((N_EVEN, D, CONV_IN_COLS), D ** -0.5),
        'conv_w_out': nrm((N_EVEN, CONV_OUT_ROWS, D), DEEPNORM_BETA * CONV_OUT_ROWS ** -0.5),
        'conv_a_dw_w': nrm((N_EVEN, CONV_A_WIDTH, CONV_A_CH), CONV_A_WIDTH ** -0.5),
        'conv_a_dw_b': nrm((N_EVEN, CONV_A_CH), 0.02),
        'conv_a_ln_g': 1.0 + nrm((N_EVEN, CONV_A_CH), 0.02),
        'conv_a_ln_b': nrm((N_EVEN, CONV_A_CH), 0.02),
        'conv_b_dw_w': nrm((N_EVEN, CONV_B_WIDTH, CONV_B_CH), CONV_B_WIDTH ** -0.5),
        'attn_w_in': nrm((N_ODD, D, ATTN_IN_COLS), D ** -0.5),
        'attn_w_out': nrm((N_ODD, ATTN_OUT_ROWS, D), DEEPNORM_BETA * ATTN_OUT_ROWS ** -0.5),
        'q_norm_g': 1.0 + nrm((N_ODD, HEAD_DIM), 0.02),
        'k_norm_g': 1.0 + nrm((N_ODD, HEAD_DIM), 0.02),
        'na_rel_bias': nrm((N_ODD, NA_HEADS, 2 * NA_WIN_ROWS - 1, 2 * NA_WIN_COLS - 1), 0.05),
        'router_w1': nrm((DEPTH, D, N_GROUPS), D ** -0.5),
        'router_b1': nrm((DEPTH, N_GROUPS), 0.01),
        'router_w2': nrm((DEPTH, D, N_EXPERTS), D ** -0.5),
        'router_b2': nrm((DEPTH, N_EXPERTS), 0.01),
        'expert_w_gate': nrm((DEPTH, N_EXPERTS, D, EXPERT_HIDDEN), D ** -0.5),
        'expert_w_up': nrm((DEPTH, N_EXPERTS, D, EXPERT_HIDDEN), D ** -0.5),
        'expert_w_down': nrm((DEPTH, N_EXPERTS, EXPERT_HIDDEN, D), DEEPNORM_BETA * EXPERT_HIDDEN ** -0.5),
    }

def first_block(x, c, ctx, c_ctx, ada_w, ada_b, ln1_g, ln1_b, ln2_g, ln2_b,
              conv_w_in, conv_w_out, conv_a_dw_w, conv_a_dw_b, conv_a_ln_g, conv_a_ln_b, conv_b_dw_w,
              attn_w_in, attn_w_out, q_norm_g, k_norm_g, na_rel_bias,
              router_w1, router_b1, router_w2, router_b2, expert_w_gate, expert_w_up, expert_w_down):
    d = x.shape[-1]
    x_lat, x_ctx = x, ctx
    for i in range(DEPTH):
        last = i == DEPTH - 1
        odd = i % 2 == 1
        j = i // 2
        sh1, sc1, g1, sh2, sc2, g2 = [m[:, None, :] for m in ada_split(c, ada_w[i], ada_b[i])]
        csh1, csc1, cg1, csh2, csc2, cg2 = ada_split(c_ctx, ada_w[i], ada_b[i])
        moe_w = (router_w1[i], router_b1[i], router_w2[i], router_b2[i],
                 expert_w_gate[i], expert_w_up[i], expert_w_down[i])
        h_lat = x_lat * (1.0 + sc1) + sh1
        h_ctx = x_ctx * (1.0 + csc1) + csh1 if (odd or not last) else None
        if odd:
            y_lat, y_ctx = attn_mixers(h_lat, h_ctx, attn_w_in[j], attn_w_out[j], q_norm_g[j], k_norm_g[j],
                                       na_rel_bias[j], not last)
        else:
            conv_w = (conv_w_in[j], conv_w_out[j], conv_a_dw_w[j], conv_a_dw_b[j],
                      conv_a_ln_g[j], conv_a_ln_b[j], conv_b_dw_w[j])
            y_lat = conv_mixers(h_lat, *conv_w)
            y_ctx = None if last else conv_mixers(h_ctx, *conv_w)
        x_lat = layer_norm(DEEPNORM_ALPHA * x_lat + g1 * y_lat, ln1_g[i], ln1_b[i])
        h_lat = x_lat * (1.0 + sc2) + sh2
        if last:
            y = hier_moe(h_lat.reshape(-1, d), *moe_w).reshape(x_lat.shape)
            x_lat = layer_norm(DEEPNORM_ALPHA * x_lat + g2 * y, ln2_g[i], ln2_b[i])
        else:
            x_ctx = layer_norm(DEEPNORM_ALPHA * x_ctx + cg1 * y_ctx, ln1_g[i], ln1_b[i])
            h_ctx = x_ctx * (1.0 + csc2) + csh2
            n_lat = h_lat.shape[0] * h_lat.shape[1]
            y = hier_moe(jnp.concatenate([h_lat.reshape(-1, d), h_ctx.reshape(-1, d)], axis=0), *moe_w)
            x_lat = layer_norm(DEEPNORM_ALPHA * x_lat + g2 * y[:n_lat].reshape(x_lat.shape), ln2_g[i], ln2_b[i])
            x_ctx = layer_norm(DEEPNORM_ALPHA * x_ctx + cg2 * y[n_lat:].reshape(x_ctx.shape), ln2_g[i], ln2_b[i])
    return x_lat


DEPTH_2 = 1

SSM_WIDTH = 512
SSM_GROUP = 16
SSM_GROUPS = SSM_WIDTH // SSM_GROUP
SSM_STATE = 64
ATT_HEADS = 8
ATT_HEAD_DIM = 64
ATT_WIDTH = ATT_HEADS * ATT_HEAD_DIM
KV_LATENT = 128
IDX_HEADS = 4
IDX_HEAD_DIM = 64
TOPK_MAX = 256
FFN_HIDDEN = ((-(-8 * D_MODEL // 3) + 255) // 256) * 256
IN_SIZES = (SSM_WIDTH, ATT_WIDTH, KV_LATENT, IDX_HEADS * IDX_HEAD_DIM, IDX_HEAD_DIM, IDX_HEADS, D_MODEL, D_MODEL)
D_IN = sum(IN_SIZES)
EPS = 1e-6


def rms_norm_2(x, g):
    xf = x.astype(jnp.float32)
    y = xf * lax.rsqrt(jnp.mean(xf * xf, axis=-1, keepdims=True) + EPS)
    return (y * g.astype(jnp.float32)).astype(x.dtype)

def split_cols(z, sizes):
    offs = []
    o = 0
    for s in sizes[:-1]:
        o += s
        offs.append(o)
    return jnp.split(z, offs, axis=-1)

def s5_branch(xs, a_re, a_im, log_dt, b_re, b_im, c_re, c_im, d_skip, w_glu, b_glu):
    bsz, seq, _ = xs.shape
    xg = xs.reshape(bsz, seq, SSM_GROUPS, SSM_GROUP)
    dt = jnp.exp(log_dt)[:, None]
    mag = jnp.exp(a_re * dt)
    ang = a_im * dt
    lb_re = mag * jnp.cos(ang)
    lb_im = mag * jnp.sin(ang)
    den = a_re * a_re + a_im * a_im
    coef_re = ((lb_re - 1.0) * a_re + lb_im * a_im) / den
    coef_im = (lb_im * a_re - (lb_re - 1.0) * a_im) / den
    bb_re = coef_re[..., None] * b_re - coef_im[..., None] * b_im
    bb_im = coef_re[..., None] * b_im + coef_im[..., None] * b_re
    bu_re = jnp.einsum('blgc,gpc->blgp', xg, bb_re)
    bu_im = jnp.einsum('blgc,gpc->blgp', xg, bb_im)
    ar = jnp.broadcast_to(lb_re, bu_re.shape)
    ai = jnp.broadcast_to(lb_im, bu_im.shape)

    def combine(e1, e2):
        a1r, a1i, b1r, b1i = e1
        a2r, a2i, b2r, b2i = e2
        nar = a1r * a2r - a1i * a2i
        nai = a1r * a2i + a1i * a2r
        nbr = a2r * b1r - a2i * b1i + b2r
        nbi = a2r * b1i + a2i * b1r + b2i
        return (nar, nai, nbr, nbi)

    _, _, s_re, s_im = lax.associative_scan(combine, (ar, ai, bu_re, bu_im), axis=1)
    y = jnp.einsum('blgp,gcp->blgc', s_re, c_re) - jnp.einsum('blgp,gcp->blgc', s_im, c_im)
    y = y.reshape(bsz, seq, SSM_WIDTH) + d_skip * xs
    y = jax.nn.gelu(y)
    z = y @ w_glu + b_glu
    val, gate = jnp.split(z, 2, axis=-1)
    return val * jax.nn.sigmoid(gate)

def dsa_branch(q, c_kv, q_idx, k_idx, w_idx, w_uk, w_uv):
    bsz, seq = q.shape[0], q.shape[1]
    topk = min(TOPK_MAX, seq // 4)
    nblk = seq // Q_BLOCK
    q_lat = jnp.einsum('blhd,chd->blhc', q, w_uk) * (ATT_HEAD_DIM ** -0.5)
    w_idx = w_idx * (IDX_HEADS ** -0.5)
    q_idx = q_idx * (IDX_HEAD_DIM ** -0.5)

    def to_blocks(t):
        return jnp.moveaxis(t.reshape((bsz, nblk, Q_BLOCK) + t.shape[2:]), 1, 0)

    key_pos = jnp.arange(seq)

    def one_block(args):
        blk, ql, qi, wi = args
        q_pos = blk * Q_BLOCK + jnp.arange(Q_BLOCK)
        rel = jax.nn.relu(jnp.einsum('bqhd,bkd->bqhk', qi, k_idx).astype(jnp.float32))
        iscore = jnp.einsum('bqhk,bqh->bqk', rel, wi.astype(jnp.float32))
        causal = key_pos[None, :] <= q_pos[:, None]
        iscore = jnp.where(causal[None], iscore, -jnp.inf)
        _, sel = lax.top_k(iscore, topk)
        valid = sel <= q_pos[None, :, None]
        c_sel = jax.vmap(lambda cb, ib: cb[ib])(c_kv, sel)
        logits = jnp.einsum('bqhc,bqkc->bhqk', ql, c_sel).astype(jnp.float32)
        logits = jnp.where(valid[:, None], logits, -jnp.inf)
        p = jax.nn.softmax(logits, axis=-1).astype(c_sel.dtype)
        return jnp.einsum('bhqk,bqkc->bqhc', p, c_sel)

    o = lax.map(one_block, (jnp.arange(nblk), to_blocks(q_lat), to_blocks(q_idx), to_blocks(w_idx)))
    o = jnp.moveaxis(o, 0, 1).reshape(bsz, seq, ATT_HEADS, KV_LATENT)
    out = jnp.einsum('blhc,chd->blhd', o, w_uv)
    return out.reshape(bsz, seq, ATT_WIDTH)

def second_inputs(seed: int = 0) -> dict:
    key = jax.random.key(seed)
    ks = jax.random.split(key, 27)
    f32 = jnp.float32

    def nrm(k, shape, s):
        return jax.random.normal(k, shape, f32) * s

    def gain(k, shape):
        return 1.0 + 0.05 * jax.random.normal(k, shape, f32)

    G, P, Cg = SSM_GROUPS, SSM_STATE, SSM_GROUP
    a_im0 = jnp.broadcast_to(jnp.pi * jnp.arange(P, dtype=f32), (DEPTH_2, G, P))
    return {
        'x': nrm(ks[0], (BATCH, SEQ, D_MODEL), 1.0),
        'c': nrm(ks[1], (BATCH, D_MODEL), 1.0),
        'w_mod': nrm(ks[2], (DEPTH_2, D_MODEL, 6 * D_MODEL), 0.5 * D_MODEL ** -0.5),
        'b_mod': nrm(ks[3], (DEPTH_2, 6 * D_MODEL), 0.01),
        'norm1_g': gain(ks[4], (DEPTH_2, D_MODEL)),
        'w_in': nrm(ks[5], (DEPTH_2, D_MODEL, D_IN), D_MODEL ** -0.5),
        'ssm_a_re': -0.5 + nrm(ks[6], (DEPTH_2, G, P), 0.01),
        'ssm_a_im': a_im0 + nrm(ks[7], (DEPTH_2, G, P), 0.01),
        'ssm_log_dt': jax.random.uniform(ks[8], (DEPTH_2, G), f32, math.log(1e-3), math.log(1e-1)),
        'ssm_b_re': nrm(ks[9], (DEPTH_2, G, P, Cg), (2 * Cg) ** -0.5),
        'ssm_b_im': nrm(ks[10], (DEPTH_2, G, P, Cg), (2 * Cg) ** -0.5),
        'ssm_c_re': nrm(ks[11], (DEPTH_2, G, Cg, P), (2 * P) ** -0.5),
        'ssm_c_im': nrm(ks[12], (DEPTH_2, G, Cg, P), (2 * P) ** -0.5),
        'ssm_d': nrm(ks[13], (DEPTH_2, SSM_WIDTH), 1.0),
        'w_ssm_glu': nrm(ks[14], (DEPTH_2, SSM_WIDTH, 2 * D_MODEL), SSM_WIDTH ** -0.5),
        'b_ssm_glu': nrm(ks[15], (DEPTH_2, 2 * D_MODEL), 0.01),
        'kv_norm_g': gain(ks[16], (DEPTH_2, KV_LATENT)),
        'idx_k_norm_g': gain(ks[17], (DEPTH_2, IDX_HEAD_DIM)),
        'w_uk': nrm(ks[18], (DEPTH_2, KV_LATENT, ATT_HEADS, ATT_HEAD_DIM), KV_LATENT ** -0.5),
        'w_uv': nrm(ks[19], (DEPTH_2, KV_LATENT, ATT_HEADS, ATT_HEAD_DIM), KV_LATENT ** -0.5),
        'w_attn_proj': nrm(ks[20], (DEPTH_2, ATT_WIDTH, D_MODEL), ATT_WIDTH ** -0.5),
        'w_out': nrm(ks[21], (DEPTH_2, D_MODEL, D_MODEL), D_MODEL ** -0.5),
        'norm2_g': gain(ks[22], (DEPTH_2, D_MODEL)),
        'w_ffn_gate': nrm(ks[23], (DEPTH_2, D_MODEL, FFN_HIDDEN), D_MODEL ** -0.5),
        'w_ffn_up': nrm(ks[24], (DEPTH_2, D_MODEL, FFN_HIDDEN), D_MODEL ** -0.5),
        'w_ffn_down': nrm(ks[25], (DEPTH_2, FFN_HIDDEN, D_MODEL), FFN_HIDDEN ** -0.5),
        'final_g': gain(ks[26], (D_MODEL,)),
    }

def second_block(x, c, w_mod, b_mod, norm1_g, w_in, ssm_a_re, ssm_a_im, ssm_log_dt, ssm_b_re, ssm_b_im, ssm_c_re, ssm_c_im, ssm_d, w_ssm_glu, b_ssm_glu, kv_norm_g, idx_k_norm_g, w_uk, w_uv, w_attn_proj, w_out, norm2_g, w_ffn_gate, w_ffn_up, w_ffn_down, final_g):
    bsz, seq, _ = x.shape
    h = x
    cond = jax.nn.silu(c)
    for layer in range(DEPTH_2):
        mod = cond @ w_mod[layer] + b_mod[layer]
        shift1, scale1, gate1, shift2, scale2, gate2 = jnp.split(mod[:, None, :], 6, axis=-1)
        u = rms_norm_2(h, norm1_g[layer]) * (1.0 + scale1) + shift1
        xs, q, ckv, qi, ki, wi, ga, gb = split_cols(u @ w_in[layer], IN_SIZES)
        y_ssm = s5_branch(xs, ssm_a_re[layer], ssm_a_im[layer], ssm_log_dt[layer], ssm_b_re[layer], ssm_b_im[layer], ssm_c_re[layer], ssm_c_im[layer], ssm_d[layer], w_ssm_glu[layer], b_ssm_glu[layer])
        y_att = dsa_branch(q.reshape(bsz, seq, ATT_HEADS, ATT_HEAD_DIM), rms_norm_2(ckv, kv_norm_g[layer]), qi.reshape(bsz, seq, IDX_HEADS, IDX_HEAD_DIM), rms_norm_2(ki, idx_k_norm_g[layer]), wi, w_uk[layer], w_uv[layer]) @ w_attn_proj[layer]
        merged = jax.nn.sigmoid(ga) * y_ssm + jax.nn.sigmoid(gb) * y_att
        h = h + gate1 * (merged @ w_out[layer])
        u2 = rms_norm_2(h, norm2_g[layer]) * (1.0 + scale2) + shift2
        ffn = (jax.nn.silu(u2 @ w_ffn_gate[layer]) * (u2 @ w_ffn_up[layer])) @ w_ffn_down[layer]
        h = h + gate2 * ffn
    return rms_norm_2(h, final_g)


def setup_inputs(seed=0):
    out = dict(first_inputs(seed))
    for name, value in second_inputs(seed + 1).items():
        if name != "x":
            out[name + "_2"] = value
    return out


def reference(
    x, c, ctx, c_ctx, ada_w, ada_b, ln1_g, ln1_b, ln2_g, ln2_b, conv_w_in, conv_w_out,
    conv_a_dw_w, conv_a_dw_b, conv_a_ln_g, conv_a_ln_b, conv_b_dw_w, attn_w_in, attn_w_out,
    q_norm_g, k_norm_g, na_rel_bias, router_w1, router_b1, router_w2, router_b2, expert_w_gate,
    expert_w_up, expert_w_down, c_2, w_mod_2, b_mod_2, norm1_g_2, w_in_2, ssm_a_re_2,
    ssm_a_im_2, ssm_log_dt_2, ssm_b_re_2, ssm_b_im_2, ssm_c_re_2, ssm_c_im_2, ssm_d_2,
    w_ssm_glu_2, b_ssm_glu_2, kv_norm_g_2, idx_k_norm_g_2, w_uk_2, w_uv_2, w_attn_proj_2,
    w_out_2, norm2_g_2, w_ffn_gate_2, w_ffn_up_2, w_ffn_down_2, final_g_2,
):
    x = first_block(
        x, c, ctx, c_ctx, ada_w, ada_b, ln1_g, ln1_b, ln2_g, ln2_b, conv_w_in, conv_w_out,
        conv_a_dw_w, conv_a_dw_b, conv_a_ln_g, conv_a_ln_b, conv_b_dw_w, attn_w_in, attn_w_out,
        q_norm_g, k_norm_g, na_rel_bias, router_w1, router_b1, router_w2, router_b2,
        expert_w_gate, expert_w_up, expert_w_down,
    )
    return second_block(
        x, c_2, w_mod_2, b_mod_2, norm1_g_2, w_in_2, ssm_a_re_2, ssm_a_im_2, ssm_log_dt_2,
        ssm_b_re_2, ssm_b_im_2, ssm_c_re_2, ssm_c_im_2, ssm_d_2, w_ssm_glu_2, b_ssm_glu_2,
        kv_norm_g_2, idx_k_norm_g_2, w_uk_2, w_uv_2, w_attn_proj_2, w_out_2, norm2_g_2,
        w_ffn_gate_2, w_ffn_up_2, w_ffn_down_2, final_g_2,
    )


_drawn_inputs = setup_inputs


def setup_inputs(seed=0):
    import zlib

    import numpy as np

    out = dict(_drawn_inputs(seed))
    spreads = {}
    factors = {'ctx': 5.836,
     'ada_b': 4.859,
     'conv_a_dw_b': 8.0,
     'conv_a_ln_g': 8.0,
     'conv_a_ln_b': 8.0,
     'q_norm_g': 8.0,
     'k_norm_g': 8.0,
     'na_rel_bias': 8.0,
     'router_b1': 8.0,
     'router_b2': 8.0,
     'b_mod_2': 5.639,
     'norm1_g_2': 6.861,
     'ssm_a_re_2': 64.0,
     'ssm_a_im_2': 64.0,
     'ssm_log_dt_2': 64.0,
     'ssm_b_re_2': 64.0,
     'ssm_b_im_2': 64.0,
     'ssm_c_re_2': 64.0,
     'ssm_c_im_2': 64.0,
     'b_ssm_glu_2': 47.168,
     'kv_norm_g_2': 8.0,
     'idx_k_norm_g_2': 8.0,
     'norm2_g_2': 3.901}
    for name, (base, spread) in spreads.items():
        noise = np.random.default_rng([zlib.crc32(name.encode()), seed]).standard_normal(out[name].shape)
        drawn = base * np.exp(spread * noise) if base else spread * noise
        out[name] = jnp.asarray(drawn.astype(out[name].dtype))
    for name, factor in factors.items():
        out[name] = (out[name] * factor).astype(out[name].dtype)
    return out
```

```python
from contextlib import ExitStack

import numpy as np

import concourse.bass as bass
from concourse import mybir

ALU = mybir.AluOpType
ACT = mybir.ActivationFunctionType
F32 = mybir.dt.float32
F32R = mybir.dt.float32r
I32 = mybir.dt.int32
AX = mybir.AxisListType.X

P = 128
D = 1024
KD = D // P
SEQ = 256
TOK = 2 * SEQ
HD = 64
HEADS = 8
NE = 32
NG = 4
HID = 512
CAP = 128
MOST = NE + 2 * TOK // CAP
CHUNKS = MOST + 8
RING = 6
SLOT = 4096
FFN = 2816
KF = FFN // P
B3 = 4992 + 1024
PART_BANKS = (6, 7, 0, 1, 4, 5, 6, 7)
TAPS = 31
PAD = TAPS // 2
ALPHA = float((2 * 2) ** 0.25)
LN_EPS = 1e-5
RMS_EPS = 1e-6
SCALE = HD ** -0.5
TOPK = 64
STATES = 16
NEG = -1e30
LOW = -3e38
ROUND = 12582912.0
TWO_PI = 6.283185
GELU_C = float(np.sqrt(2.0 / np.pi))

PARAM = dict(cond=16, cond2=8, ada_b0=48, ada_b1=48, b_mod=48, ln1_g=16, ln1_b=16, ln2_g=16, ln2_b=16,
             dw_b=4, cln_g=4, cln_b=4, dwa=4 * TAPS, dwb=12, norm1=8, norm2=8, final=8, ssm_d=4, b_glu=16,
             a_re=16, a_im=16, log_dt=16, b_re=256, b_im=256, c_re=256, c_im=256,
             kv_g=128, ki_g=64, q_g=64, k_g=64, rb=72, rw=576, w_uk=512, w_uv=512)
CONST = dict(ident=128, before=128, iota=SEQ, cos=64, sin=64, window=64, causal=512, rev=32, rev4=4, parity=2)


def places(widths):
    at, out = 0, {}
    for name, width in widths.items():
        out[name] = (at, width)
        at += width
    return out, at


PARAM_AT, PARAM_W = places(PARAM)
CONST_AT, CONST_W = places(CONST)


class Count:

    def __init__(self, sem):
        self.sem, self.n = sem, 0

    def __call__(self, ins):
        self.n += 1
        return ins.then_inc(self.sem, 1)


def weight_chunks(w):
    def rows(ap, c0, c1, k0=0, k1=None):
        v = ap.rearrange("(k p) n -> p k n", p=P)
        return v[:, k0:(k1 or v.shape[1]), c0:c1]

    def cols(ap, edges):
        return [rows(ap, a, b) for a, b in zip(edges, edges[1:])]

    six = list(range(0, 6 * D + 1, 512))
    before = [rows_ for i in (0, 1) for rows_ in cols(w["ada_w"][i], six)] + cols(w["w_mod_2"][0], six)
    before += cols(w["conv_w_in"][0], range(0, 2561, 512)) + cols(w["conv_w_out"][0], [0, 512, 1024])
    middle = cols(w["attn_w_in"][0], [0, 512, 768, 1280, 1792, 2304]) + cols(w["attn_w_out"][0], [0, 512, 1024])
    after = cols(w["w_in_2"][0], [0, 512, 1024, 1476, 1988, 2500, 3012, 3524])
    after += cols(w["w_ssm_glu_2"][0], [0, 1024, 2048]) + cols(w["w_attn_proj_2"][0], [0, 1024])
    after += cols(w["w_out_2"][0], [0, 512, 1024])
    edges = list(range(0, FFN, 512)) + [FFN]
    for a, b in zip(edges, edges[1:]):
        after += [rows(w["w_ffn_gate_2"][0], a, b), rows(w["w_ffn_up_2"][0], a, b)]
    after += [rows(w["w_ffn_down_2"][0], 0, D, k, min(k + 4, KF)) for k in range(0, KF, 4)]
    return before, middle, after


def two_blocks(nc, w, out):
    before, middle, after = weight_chunks(w)
    per_moe = 3 * NE
    start = {"before": 0, "moe0": len(before), "middle": len(before) + per_moe}
    start["moe1"] = start["middle"] + len(middle)
    start["after"] = start["moe1"] + per_moe

    with ExitStack() as ctx:
        def sb(name, width, dt=F32):
            where[name] = -(-nc.sbuf_base // 32) * 32 + sum(widths.values()) * 4
            widths[name] = -(-width // 8) * 8
            return nc.alloc_sbuf_tensor_at(name, [P, width], dt, offset=where[name])

        def rounded(name, of, first, width):
            return nc.alloc_sbuf_tensor_at(name, [P, width], F32R, offset=where[of] + 4 * first)

        where, widths = {}, {}

        sems = {}

        def sem(name):
            if name not in sems:
                sems[name] = ctx.enter_context(nc.semaphore(name))
            return sems[name]

        ring = sb("ring", RING * SLOT)
        x_t = sb("x_t", KD * TOK)
        h_t = sb("h_t", KD * TOK)
        b12 = sb("b12", 8192)
        b3 = sb("b3", B3)
        par = sb("par", PARAM_W)
        con = sb("con", CONST_W)
        ones_d = sb("ones_d", P)
        ones_c = sb("ones_c", P)
        ones_m = sb("ones_m", P)
        mods = sb("mods", 96 + 96 + 48)
        sm = sb("sm", 392)
        owner = sb("owner", CHUNKS, I32)
        cum = sb("cum", NE + 1 + 7, I32)
        bank = [ctx.enter_context(nc.psum_tensor(f"bank{i}", [P, 512], F32)) for i in range(8)]
        V_BANKS, A_BANKS = bank[:4], bank[4:]

        def v3(t, off, a, b):
            return t[:, off:off + a * b].rearrange("p (a b) -> p a b", a=a)

        def v4(t, off, a, b, c):
            return t[:, off:off + a * b * c].rearrange("p (a b c) -> p a b c", a=a, b=b)

        def pr(name, i=0, n=None):
            a, width = PARAM_AT[name]
            return par[:, a + i:a + (width if n is None else i + n)]

        def cn(name, i=0, n=None):
            a, width = CONST_AT[name]
            return con[:, a + i:a + (width if n is None else i + n)]

        X = v3(x_t, 0, KD, TOK)
        H = v3(h_t, 0, KD, TOK)
        ident = cn("ident")
        cond_s = v3(sm, 0, 8, 2)
        cond2_s = sm[:, 16:24]
        MOD = [v3(mods, 0, 48, 2), v3(mods, 96, 48, 2), v3(mods, 192, 48, 1)]

        def mod(i, part, k, src):
            return MOD[i][:, part * 8 + k, src:src + 1]

        def chunk(n, k, cols):
            return v3(ring, (n % RING) * SLOT, k, cols)

        v_full, v_free, a_full, a_free = sem("v_full"), sem("v_free"), sem("a_full"), sem("a_free")
        slot_loaded = [sem(f"slot_loaded{i}") for i in range(RING)]
        marks = {}
        read_by = {}

        tok_in = v3(b12, 0, 4, D)
        mod_rows = b12[:, 0:6 * D]
        a_val, a_sig = v3(b12, 0, 4, TOK), v3(b12, 2048, 4, TOK)
        conv_y = v3(b12, 0, 8, TOK)
        b_gate, c_gate = v3(b12, 4096, 4, TOK), v3(b12, 6144, 4, TOK)
        PW, QW = SEQ + 2 * PAD, SEQ + 2
        ya_pad, cb_pad = v4(b3, 0, 4, 2, PW), v4(b3, 4 * 2 * PW, 4, 2, QW)
        ln_sq = b12[:, 4096:8192]
        ln_s = [b3[:, 4 * 2 * PW + 512 * i:4 * 2 * PW + 512 * (i + 1)] for i in range(3)]
        h_lo_full, acc = v3(b12, 4096, 4, D), H
        h_hi, h_lo = v3(rounded("h_hi", "b12", 0, 4096), 0, 4, D), v3(rounded("h_lo", "b12", 4096, 4096), 0, 4, D)
        disp, comb = v3(rounded("disp", "b3", 0, 512), 0, 4, CAP), v3(b3, 512, 4, CAP)
        xe, comb_t = v3(b3, 1024, KD, CAP), rounded("comb_t", "b3", 2048, 512)[:, :]
        silu_g, hid = b3[:, 2560:3072], v3(b3, 3072, 4, CAP)
        xe_rows, y_hi = b3[:, 3584:4608], rounded("y_hi", "b3", 3584, 1024)[:, :]
        y_lo = rounded("y_lo", "b3", 4992, 1024)[:, :]
        h_hi_f, disp_f, y_hi_f = [t.bitcast(F32) for t in (h_hi, disp, y_hi)]
        rank, gates, small = v3(b3, 4608, 4, NE), v3(b3, 4736, 4, NE), b3[:, 4864:4992]
        place, slot_gate, per_chunk = small[:, 0:4], small[:, 4:5], small[:, 80:80 + CHUNKS]
        route = v3(b3, 1024, 4, 36)
        sel, one1, one2, tmp32, ml = [v3(b3, 1168 + 128 * i, 4, NE) for i in range(5)]
        nch = [b3[:, 1808 + 32 * i:1840 + 32 * i] for i in range(3)]
        q_tok, kv_tok, kd_t = v3(b12, 0, 2, 512), v3(b12, 1024, 4, 256), v3(b12, 2048, 4, TOK)
        vd_tok, qd_t, qc_t = v3(b12, 4096, 4, 512), v3(b12, 6144, 4, SEQ), v3(b12, 7168, 4, SEQ)
        kc_t = v3(b3, 0, 2, TOK)
        prob = [b3[:, 1024 + 512 * i:1536 + 512 * i] for i in range(2)]
        prob_t = [v3(b3, 2048 + 512 * i, 4, P) for i in range(2)]
        bias = [v3(b3, 3072 + 512 * i, 2, SEQ) for i in range(2)]
        logit = [b3[:, 4096 + 512 * i:4608 + 512 * i] for i in range(2)]
        o_tok, o_t = v3(h_t, 0, 2, D), v3(h_t, 2048, KD, SEQ)
        y_gated = v3(b12, 4096, KD, SEQ)
        kdup = v4(b3, 4096, 4, 2, P)
        st = sm[:, 64:392]
        X2 = X[:, :, 0:SEQ]
        U = v3(h_t, 0, KD, SEQ)
        xs_t, q2_t, sga = v3(b12, 0, 4, SEQ), v3(b12, 1024, 4, SEQ), v3(b12, 2048, KD, SEQ)
        sgb, misc = v3(b12, 4096, KD, SEQ), v3(b12, 6144, 2, 452)
        qi_t, ckv_t, ki_t = v3(b12, 7048, 2, SEQ), b12[:, 7560:7816], b12[:, 7816:8072]
        def s5w(i):
            return X[:, i // 2, SEQ + P * (i % 2):SEQ + P * (i % 2) + P]
        cos_t, sin_t, u_re, u_im = [v3(h_t, 1024 * i, 4, SEQ) for i in range(4)]
        z_re, z_im, t_a, t_b = [v3(b3, 1024 * i, 4, SEQ) for i in range(4)]
        y_ssm = v3(b3, 4096, 4, SEQ)
        val, sig = v3(h_t, 0, KD, SEQ), v3(h_t, 2048, KD, SEQ)
        def expanded(i):
            return b3[:, 2048 + P * (i % 4):2048 + P * (i % 4) + P]
        ki_dup = [b3[:, 256 + P * t:256 + P * t + P] for t in range(2)]
        isc, work, ties, relu = [b3[:, 256 * i:256 * (i + 1)] for i in range(4)]
        mask = v3(b3, 1024, 2, SEQ)
        p2 = [b3[:, 1536 + 256 * i:1792 + 256 * i] for i in range(2)]
        p2_t = [v3(b3, 2048 + 256 * i, 2, P) for i in range(2)]
        q_lat = [b3[:, 2560 + 256 * i:2816 + 256 * i] for i in range(2)]
        lat_o = [b3[:, 3072 + 256 * i:3328 + 256 * i] for i in range(2)]
        wuk_t = v3(b3, 3584, 4, P)
        atto = v3(h_t, 0, 4, SEQ)
        relu4 = [v3(h_t, 1024 + 1024 * t, 4, SEQ) for t in range(2)]
        f_hid = v3(b12, 0, KF, SEQ)
        f_sil = v3(b3, 0, 4, SEQ)
        fin = v3(b12, 0, 2, D)

        block = ctx.enter_context(nc.Block())

        @block.tensor
        def _(pe):
            lane = {"v": 0, "a": 0}

            def group(which, emit, b=None):
                n = lane[which]
                full, free, banks = (v_full, v_free, V_BANKS) if which == "v" else (a_full, a_free, A_BANKS)
                if n >= 4:
                    pe.wait_ge(free, n - 3)
                emit(banks[n % 4]).then_inc(full, 1)
                lane[which] = n + 1

            def taken():
                pe.wait_ge(v_free, lane["v"])
                if lane["a"]:
                    pe.wait_ge(a_free, lane["a"])

            def loaded(n):
                pe.wait_ge(slot_loaded[n % RING], 16 * (n // RING + 1))

            def done_with(n):
                read_by[n] = (lane["v"], lane["a"])

            def mark(name):
                marks[name] = (lane["v"], lane["a"])

            def sum_k(o, lhs, rhs, nk):
                for k in range(nk):
                    last = pe.matmul(o, lhs(k), rhs(k), start=(k == 0), stop=(k == nk - 1))
                return last

            def modulation(n0, cond, width):
                for j in range(12):
                    loaded(n0 + j)
                    wt = chunk(n0 + j, KD, 512)
                    group("va"[j % 2], lambda b: sum_k(b[0:width, :], cond, lambda k: wt[:, k, :], KD))
                    done_with(n0 + j)
                taken()
                group("v", lambda b: transposes(b, [(width * m, mod_rows[0:width, m * P:(m + 1) * P]) for m in range(48)]))

            def channel_out(n, lanes, rhs, nk, ncols, ntok):
                loaded(n)
                wt = chunk(n, nk, ncols)
                for m in range(ncols // P):
                    group(lanes[m % len(lanes)],
                          lambda b: sum_k(b[:, 0:ntok], lambda k: wt[:, k, m * P:(m + 1) * P], rhs, nk))
                done_with(n)

            def token_out(n, which, lhs, tiles, ncols):
                loaded(n)
                wt = chunk(n, KD, ncols)
                for t in range(tiles):
                    group(which, lambda b: sum_k(b[:, 0:ncols], lambda k: lhs(k, t), lambda k: wt[:, k, :], KD))
                done_with(n)

            def norm_sums(name, ones, ntok, rounds=2):
                for i in range(rounds):
                    pe.wait_ge(sem(f"{name}_sum{i}"), 1)
                    group("v", lambda b: pe.matmul(b[:, 0:ntok], ones, ln_s[0][:, 0:ntok], start=True, stop=True))
                mark(name)

            def transposes(b, pieces):
                for o, i in pieces:
                    last = pe.transpose(b[0:i.shape[-1], o:o + i.shape[0]], i, ident[0:i.shape[0], 0:i.shape[0]])
                return last

            def moe(layer, tiles):
                n0 = start[f"moe{layer}"]
                ntok = tiles * P
                pe.wait_ge(sem(f"h2_v{layer}"), 1)
                if layer == 0:
                    pe.wait_ge(sem(f"h2_a{layer}"), 1)

                def logits(b):
                    rw = v3(par, PARAM_AT["rw"][0] + 288 * layer, KD, 36)
                    for t in range(tiles):
                        last = sum_k(b[:, 36 * t:36 * t + 36], lambda k: H[:, k, t * P:(t + 1) * P],
                                     lambda k: rw[:, k, :], KD)
                    return last
                group("v", logits)
                for t in range(tiles):
                    for half in range(2):
                        group("a", lambda b: transposes(b, [
                            (P * kk, H[:, 4 * half + kk, t * P:(t + 1) * P]) for kk in range(4)]))
                pe.wait_ge(sem(f"chosen{layer}"), 1)

                def ranks(b):
                    for t in range(tiles + 1):
                        for s in range(min(t + 1, tiles)):
                            tri = cn("before") if s == t else ones_c[:, :]
                            last = pe.matmul(b[:, NE * t:NE * t + NE], tri, sel[:, s, :],
                                             start=(s == 0), stop=(s == min(t, tiles - 1)))
                    return last
                group("v", ranks)
                taken()
                s = {k: sem(f"{k}{layer}") for k in ("dispatch_ready", "combine_ready", "rows_full", "rows_taken",
                                                      "xe_full", "xe_taken", "gt_full", "gt_taken", "gate_full",
                                                      "up_full", "hid_ready", "y_full", "hi_ready", "lo_ready",
                                                      "part_full", "part_added")}
                pe.wait_ge(sem(f"h_split{layer}"), 1)
                pe.wait_ge(sem(f"table_ready{layer}"), 1)
                pe.sem_inc(s["rows_full"], 2)
                pe.sem_inc(s["gt_full"], 1)

                def dispatch(n):
                    pe.wait_ge(s["dispatch_ready"], n + 1)
                    pe.wait_ge(s["xe_taken"], n + 1)
                    for half in range(2):
                        for part in (h_hi, h_lo):
                            for t in range(tiles):
                                last = pe.matmul(bank[half][:, :], disp[:, t, :],
                                                 part[:, t, half * 512:(half + 1) * 512],
                                                 start=(part is h_hi and t == 0), stop=(part is h_lo and t == tiles - 1))
                        last.then_inc(s["rows_full"], 1)

                def turn(n):
                    pe.wait_ge(s["rows_taken"], n + 1)
                    for half in range(2):
                        last = transposes(bank[half], [(P * k, xe_rows[:, (4 * half + k) * P:(4 * half + k + 1) * P])
                                                       for k in range(4)])
                    last.then_inc(s["xe_full"], 1)

                dispatch(0)
                turn(0)
                with pe.Fori(0, NE // 2) as pair:
                    for j in range(2):
                        e = pair * 2 + j
                        cs = [n0 + 3 * j + i for i in range(3)]
                        wg, wu, wd = chunk(cs[0], KD, HID), chunk(cs[1], KD, HID), chunk(cs[2], 4, D)
                        for c in cs:
                            pe.wait_ge(slot_loaded[c % RING], pair * 16 + 16 * (c // RING + 1))
                        trips = pe.value_load(cum[0:1, bass.ds(e + 1, 1)], min_val=1, max_val=MOST)
                        if j == 0:
                            first = pe.value_load(cum[0:1, bass.ds(e, 1)], min_val=0, max_val=MOST)
                        else:
                            first = first_trips
                        first_trips = trips
                        with pe.Fori(first, trips) as n:
                            pe.wait_ge(s["xe_taken"], n + 2)
                            pe.wait_ge(s["hid_ready"], n + 1)
                            for wt, b, name in ((wg, bank[3], "gate_full"), (wu, bank[2], "up_full")):
                                for m in range(4):
                                    for k in range(KD):
                                        last = pe.matmul(b[:, m * CAP:(m + 1) * CAP], wt[:, k, m * P:(m + 1) * P],
                                                         xe[:, k, :], start=(k == 0), stop=(k == KD - 1))
                                last.then_inc(s[name], 1)
                            pe.wait_ge(s["part_added"], n * KD + KD)
                            dispatch(n + 1)
                            pe.wait_ge(s["hid_ready"], n + 2)
                            pe.wait_ge(s["combine_ready"], n + 1)
                            for t in range(tiles):
                                last = pe.transpose(bank[3][:, t * P:(t + 1) * P], comb[:, t, :], ident)
                            last.then_inc(s["gt_full"], 1)
                            for half in range(2):
                                for k in range(4):
                                    last = pe.matmul(bank[4 + half][:, :], hid[:, k, :],
                                                     wd[:, k, half * 512:(half + 1) * 512], start=(k == 0), stop=(k == 3))
                                last.then_inc(s["y_full"], 1)
                                if half == 0:
                                    turn(n + 1)
                            pe.wait_ge(s["gt_taken"], n + 1)
                            for k in range(KD):
                                if k % 4 == 0:
                                    pe.wait_ge(s["hi_ready"], n * 2 + k // 4 + 1)
                                    pe.wait_ge(s["lo_ready"], n * 2 + k // 4 + 1)
                                    if k == 0:
                                        pe.wait_ge(s["xe_taken"], n + 2)
                                if k >= 6:
                                    pe.wait_ge(s["part_added"], n * KD + k + 3)
                                b = bank[PART_BANKS[k]][:, 0:ntok]
                                pe.matmul(b, y_hi[:, k * P:(k + 1) * P], comb_t[:, 0:ntok], start=True, stop=False)
                                pe.matmul(b, y_lo[:, k * P:(k + 1) * P], comb_t[:, 0:ntok], start=False, stop=True) \
                                    .then_inc(s["part_full"], 1)

            pe.wait_ge(sem("consts"), 16)
            pe.wait_ge(sem("x_in"), 64)
            pe.wait_ge(sem("ones"), 3)
            for k in range(KD):
                group("va"[k % 2], lambda b: transposes(b, [(P * t, tok_in[:, t, k * P:(k + 1) * P]) for t in range(4)]))
            pe.wait_ge(sem("cond_ready"), 2)
            modulation(0, lambda k: cond_s[:, k, :], 2)
            modulation(12, lambda k: cond_s[:, k, :], 2)
            modulation(24, lambda k: cond2_s[:, k:k + 1], 1)

            mark("mods")

            pe.wait_ge(sem("h_v0"), 1)
            pe.wait_ge(sem("h_a0"), 1)
            n = 36
            for j, which in enumerate("vaaav"):
                channel_out(n + j, which, lambda k: H[:, k, :], KD, 512, TOK)
            n += 5
            norm_sums("cln", ones_m[:, :], TOK)
            pe.wait_ge(sem("conv_ya"), 1)
            pe.wait_ge(sem("conv_yb"), 1)
            for j in range(2):
                channel_out(n + j, "a", lambda k: conv_y[:, k, :], KD, 512, TOK)
            mark("y_conv")
            norm_sums("ln0", ones_d[:, :], TOK)
            moe(0, 4)
            norm_sums("ln1", ones_d[:, :], TOK)

            pe.wait_ge(sem("h_v1"), 1)
            pe.wait_ge(sem("h_a1"), 1)
            n = start["middle"]
            token_out(n, "v", lambda k, t: H[:, k, t * P:(t + 1) * P], 2, 512)
            token_out(n + 1, "v", lambda k, t: H[:, k, t * P:(t + 1) * P], 4, 256)
            channel_out(n + 2, "a", lambda k: H[:, k, 0:SEQ], KD, 512, SEQ)
            channel_out(n + 3, "a", lambda k: H[:, k, :], KD, 512, TOK)
            token_out(n + 4, "a", lambda k, t: H[:, k, t * P:(t + 1) * P], 4, 512)
            mark("attention_in")
            pe.wait_ge(sem("rope_done"), 1)
            for j in range(4):
                group("v", lambda b: transposes(b, [(P * t, q_tok[:, t, j * P:(j + 1) * P]) for t in range(2)]))
            for j in range(2):
                group("v", lambda b: transposes(b, [(P * t, kdup[:, t, j, :]) for t in range(4)]))
            taken()

            def scores(u):
                kind, h, t = u // 16, (u % 16) // 2, u % 2
                if u >= 2:
                    pe.wait_ge(sem("exp_done"), u - 1)
                p0 = HD * (h % 2)
                if kind == 0:
                    q, k = qc_t[p0:p0 + HD, h // 2, t * P:(t + 1) * P], kc_t[p0:p0 + HD, h // 4, :]
                else:
                    q, k = qd_t[p0:p0 + HD, h // 2, t * P:(t + 1) * P], kd_t[p0:p0 + HD, h // 2, :]
                pe.matmul(bank[u % 2][:, :], q, k, start=True, stop=True).then_inc(sem("score_full"), 1)

            def weigh(u):
                kind, h, t = u // 16, (u % 16) // 2, u % 2
                pe.wait_ge(sem("exp_done"), u + 1)
                if u >= 2:
                    pe.wait_ge(sem("pt_taken"), u - 1)
                transposes(bank[2 + u % 2], [(P * k, prob[u % 2][:, k * P:(k + 1) * P]) for k in range(4)]) \
                    .then_inc(sem("pt_full"), 1)

            def mix(u):
                kind, h, t = u // 16, (u % 16) // 2, u % 2
                pe.wait_ge(sem("pt_taken"), u + 1)
                if u >= 2:
                    pe.wait_ge(sem("o_taken"), u - 1)
                v = kv_tok if kind == 0 else vd_tok
                c = P + HD * (h // 4) if kind == 0 else h * HD
                sum_k(bank[4 + u % 2][:, 0:HD], lambda k: prob_t[u % 2][:, k, :], lambda k: v[:, k, c:c + HD], 4) \
                    .then_inc(sem("o_full"), 1)

            scores(0)
            for u in range(32):
                if u < 31:
                    scores(u + 1)
                if u:
                    mix(u - 1)
                weigh(u)
            mix(31)
            pe.wait_ge(sem("o_taken"), 32)
            for k in range(KD):
                group("va"[k % 2], lambda b: transposes(b, [(P * t, o_tok[:, t, k * P:(k + 1) * P]) for t in range(2)]))
            taken()
            for j in range(2):
                channel_out(n + 5 + j, "a", lambda k: o_t[:, k, :], KD, 512, SEQ)
            mark("y_attn")
            norm_sums("ln2", ones_d[:, :], SEQ)
            moe(1, 2)
            norm_sums("ln3", ones_d[:, :], SEQ)

            norm_sums("rms1", ones_d[:, :], SEQ, 1)
            for i in range(16):
                pe.wait_ge(sem("s5_expanded"), i + 1)
                group("v", lambda b: transposes(b, [(0, expanded(i))]))
            pe.wait_ge(sem("u1_ready"), 1)
            n = start["after"]
            channel_out(n, "v", lambda k: U[:, k, :], KD, 512, SEQ)
            channel_out(n + 1, "a", lambda k: U[:, k, :], KD, 512, SEQ)
            token_out(n + 2, "v", lambda k, t: U[:, k, t * P:(t + 1) * P], 2, 452)
            for j in range(4):
                channel_out(n + 3 + j, "a", lambda k: U[:, k, :], KD, 512, SEQ)
            mark("in_proj")
            taken()
            for i in range(4):
                for im in range(2):
                    for jj in range(4):
                        group("v", lambda b: pe.matmul(b[:, 0:SEQ], s5w(4 * im + i)[32 * jj:32 * jj + 32, :],
                                                       xs_t[32 * jj:32 * jj + 32, i, :], start=True, stop=True))
                pe.wait_ge(sem("scan_done"), i + 1)

                def read_out(b):
                    for jj in range(4):
                        for im, z in ((0, z_re), (1, z_im)):
                            last = pe.matmul(b[32 * jj:32 * jj + 32, 0:SEQ], s5w(8 + 4 * im + i)[:, 32 * jj:32 * jj + 32],
                                             z[:, jj, :], start=(im == 0), stop=(im == 1), tile_position=(0, 32 * jj))
                    return last
                group("v", read_out)
            pe.wait_ge(sem("y_gelu"), 1)
            for j in range(2):
                channel_out(n + 7 + j, "a", lambda k: y_ssm[:, k, :], 4, 1024, SEQ)
            mark("glu")
            pe.wait_ge(sem("dsa_norm"), 1)
            for t in range(2):
                group("v", lambda b: transposes(b, [(0, misc[:, t, 0:P])]))
                group("v", lambda b: transposes(b, [(0, ki_dup[t])]))
                for j in range(2):
                    group("v", lambda b: transposes(b, [(0, misc[:, t, P + j * P:2 * P + j * P])]))
            for j in range(4):
                group("v", lambda b: transposes(b, [(0, pr("w_uk", j * P, P))]))
            taken()
            for t in range(2):
                for hh in range(4):
                    p0 = HD * (hh % 2)
                    group("a", lambda b: pe.matmul(b[:, 0:SEQ], qi_t[p0:p0 + HD, hh // 2, t * P:(t + 1) * P],
                                                   ki_t[p0:p0 + HD, :], start=True, stop=True))
            for h in range(HEADS):
                p0 = HD * (h % 2)
                if h == 0:
                    mark("heads")
                group("v", lambda b: pe.matmul(b[:, 0:SEQ], wuk_t[p0:p0 + HD, h // 2, :], q2_t[p0:p0 + HD, h // 2, :],
                                               start=True, stop=True))
                pe.wait_ge(v_free, lane["v"])
                for t in range(2):
                    u = 2 * h + t
                    group("v", lambda b: pe.matmul(b[:, 0:SEQ], q_lat[h % 2][:, t * P:(t + 1) * P], ckv_t,
                                                   start=True, stop=True))
                    pe.wait_ge(sem("p2_ready"), u + 1)
                    group("a", lambda b: transposes(b, [(P * k, p2[t][:, k * P:(k + 1) * P]) for k in range(2)]))
                    pe.wait_ge(a_free, lane["a"])
                    group("v", lambda b: sum_k(b[:, 0:P], lambda k: misc[:, k, 0:P], lambda k: p2_t[t][:, k, :], 2))
                pe.wait_ge(v_free, lane["v"])
                group("a", lambda b: pe.matmul(b[p0:p0 + HD, 0:SEQ], pr("w_uv", h * HD, HD), lat_o[h % 2],
                                               start=True, stop=True, tile_position=(0, p0)))
            taken()
            channel_out(n + 9, "v", lambda k: atto[:, k, :], 4, 1024, SEQ)
            pe.wait_ge(sem("merged"), 1)
            for j in range(2):
                channel_out(n + 10 + j, "a", lambda k: sga[:, k, :], KD, 512, SEQ)
            mark("y_block2")
            norm_sums("rms2", ones_d[:, :], SEQ, 1)
            pe.wait_ge(sem("u2_ready"), 1)
            mark("ffn")
            for j in range(6):
                cols = min(512, FFN - 512 * j)
                channel_out(n + 12 + 2 * j, "a", lambda k: U[:, k, :], KD, cols, SEQ)
                channel_out(n + 13 + 2 * j, "v", lambda k: U[:, k, :], KD, cols, SEQ)
            taken()
            for c in range(6):
                loaded(n + 24 + c)
                ks = range(4 * c, min(4 * c + 4, KF))
                wt = chunk(n + 24 + c, len(ks), D)
                for kk, k in enumerate(ks):
                    for m in range(KD):
                        last = pe.matmul(bank[m][:, 0:SEQ], wt[:, kk, m * P:(m + 1) * P], f_hid[:, k, :],
                                         start=(k == 0), stop=(k == KF - 1))
                        if k == KF - 1:
                            last.then_inc(sem("down_full"), 1)
            pe.wait_ge(sem("rms3_sum0"), 1)
            pe.matmul(bank[0][:, 0:SEQ], ones_d[:, :], ln_s[0][:, 0:SEQ], start=True, stop=True).then_inc(sem("rms3_full"), 1)
            pe.wait_ge(sem("final_ready"), 1)
            for t in range(2):
                for half in range(2):
                    b = bank[1 + 2 * t + half]
                    transposes(b, [(P * kk, X2[:, 4 * half + kk, t * P:(t + 1) * P]) for kk in range(4)]) \
                        .then_inc(sem("final_full"), 1)

        @block.vector
        def _(dv):
            step = Count(sem("dve_step"))
            taken = Count(v_free)

            def done():
                if step.n:
                    dv.wait_ge(step.sem, step.n)
                if taken.n:
                    dv.wait_ge(v_free, taken.n)

            def full():
                dv.wait_ge(v_full, taken.n + 1)
                return V_BANKS[taken.n % 4]

            def do(ins):
                step(ins)
                done()

            def tt(o, a, b, op):
                return dv.tensor_tensor(o, a, b, op)

            def modulation(i, bias_name):
                width = 2 if i < 2 else 1
                for j in range(0, 12, 2):
                    b = full()
                    taken(dv.tensor_copy(mod_rows[0:width, j * 512:(j + 1) * 512], b[0:width, :]))
                b = full()
                taken(tt(MOD[i], v3(b, 0, 48, width), pr(bias_name).unsqueeze(2).broadcast_to([P, 48, width]), ALU.add))
                done()
                for part in (1, 4):
                    m = MOD[i][:, 8 * part:8 * part + 8, :]
                    step(dv.tensor_scalar(m, m, 1.0, None, ALU.add))
                done()

            def modulate(i, part, event):
                for k in range(KD):
                    ins = dv.tensor_scalar(H[:, k, 0:SEQ], X[:, k, 0:SEQ], mod(i, part + 1, k, 0), mod(i, part, k, 0),
                                           ALU.mult, ALU.add)
                ins.then_inc(sem(event), 1)
                dv.wait_ge(sem(event), 1)

            def k_sum(o, t, ntok):
                return dv.tensor_reduce(o, t.rearrange("p k n -> p n k"), AX, ALU.add)

            def layer_norm(name, z, nk, ntok, sq, event):
                s = [x[:, 0:ntok] for x in ln_s]
                k_sum(s[0], z, ntok).then_inc(sem(f"{name}_sum0"), 1)
                b = full()
                taken(tt(z, z, b[:, 0:ntok].unsqueeze(1).broadcast_to([P, nk, ntok]), ALU.subtract))
                done()
                do(tt(sq, z, z, ALU.mult))
                k_sum(s[0], sq, ntok).then_inc(sem(f"{name}_sum1"), 1)
                b = full()
                taken(dv.tensor_scalar(s[1], b[:, 0:ntok], LN_EPS, None, ALU.add))
                dv.wait_ge(sem(f"{name}_root"), 1)
                do(dv.reciprocal(s[1], s[2]))
                tt(z, z, s[1].unsqueeze(1).broadcast_to([P, nk, ntok]), ALU.mult).then_inc(sem(event), 1)

            def moe(layer, tiles):
                ntok = tiles * P
                b = full()
                rb = pr("rb", 36 * layer, 36).unsqueeze(1).broadcast_to([P, tiles, 36])
                taken(tt(route[:, 0:tiles, :], v3(b, 0, tiles, 36), rb, ALU.add))
                done()
                l1, l2 = route[:, 0:tiles, 0:NG], route[:, 0:tiles, NG:36]
                g = [small[:, 4 * i:4 * i + tiles].unsqueeze(2) for i in range(8)]
                four = [v3(small, 32 + 16 * i, 4, NG)[:, 0:tiles, :] for i in range(3)]
                to4 = lambda a: a.broadcast_to([P, tiles, NG])
                to32 = lambda a: a.broadcast_to([P, tiles, NE])
                fl = lambda a: a.rearrange("p t o -> p (t o)")

                def first_max(o, vals, top, rev, n, wide):
                    do(dv.tensor_reduce(fl(top), vals, AX, ALU.max))
                    do(tt(o, vals, wide(top), ALU.is_equal))
                    do(tt(o, o, rev.unsqueeze(1).broadcast_to([P, tiles, n]), ALU.mult))
                    do(dv.tensor_reduce(fl(g[7]), o, AX, ALU.max))
                    do(tt(o, o, wide(g[7]), ALU.is_equal))

                first_max(four[0], l1, g[0], cn("rev4"), NG, to4)
                tt(four[1], l1, to4(g[0]), ALU.subtract).then_inc(sem(f"group_shift{layer}"), 1)
                dv.wait_ge(sem(f"group_exp{layer}"), 1)
                do(dv.tensor_reduce(fl(g[1]), four[2], AX, ALU.add))
                oh = four[0].unsqueeze(3).broadcast_to([P, tiles, NG, 8])
                m = ml[:, 0:tiles, :]
                m4 = m.rearrange("p t (g e) -> p t g e", g=NG)
                l24 = l2.rearrange("p t (g e) -> p t g e", g=NG)
                for t in range(tiles):
                    step(tt(m4[:, t], l24[:, t], oh[:, t], ALU.mult))
                do(dv.tensor_scalar(four[1], four[0], -1.0, -NEG, ALU.add, ALU.mult))
                oh = four[1].unsqueeze(3).broadcast_to([P, tiles, NG, 8])
                for t in range(tiles):
                    step(tt(m4[:, t], m4[:, t], oh[:, t], ALU.add))
                done()
                o1, o2, tm = one1[:, 0:tiles, :], one2[:, 0:tiles, :], tmp32[:, 0:tiles, :]
                first_max(o1, m, g[2], cn("rev"), NE, to32)
                do(dv.tensor_scalar(tm, o1, 4 * NEG, None, ALU.mult))
                do(tt(m, m, tm, ALU.add))
                first_max(o2, m, g[3], cn("rev"), NE, to32)
                tt(g[4], g[3], g[2], ALU.subtract).then_inc(sem(f"pair_shift{layer}"), 1)
                sl = sel[:, 0:tiles, :]
                dv.wait_ge(sem(f"pair_shift{layer}"), 1)
                tt(sl, o1, o2, ALU.add).then_inc(sem(f"chosen{layer}"), 1)
                dv.wait_ge(sem(f"pair_exp{layer}"), 1)
                do(dv.tensor_scalar(g[6], g[5], 1.0, None, ALU.add))
                do(tt(g[6], g[6], g[1], ALU.mult))
                do(dv.reciprocal(fl(g[6]), fl(g[6])))
                do(tt(g[5], g[5], g[6], ALU.mult))
                dv.wait_ge(sem(f"h_copied{layer}"), 2 * tiles)
                for t in range(tiles):
                    ins = tt(h_lo[:, t, :], h_lo_full[:, t, :], h_hi_f[:, t, :], ALU.subtract)
                ins.then_inc(sem(f"h_split{layer}"), 1)
                gt = gates[:, 0:tiles, :]
                do(tt(gt, o1, to32(g[6]), ALU.mult))
                do(tt(tm, o2, to32(g[5]), ALU.mult))
                do(tt(gt, gt, tm, ALU.add))
                b = full()
                rk = rank[:, 0:tiles, :]
                step(dv.tensor_scalar(rk, v3(b, 0, tiles, NE), 1.0, None, ALU.add))
                taken(dv.tensor_copy(nch[0], b[:, NE * tiles:NE * (tiles + 1)]))
                done()
                dv.wait_ge(sem(f"chosen{layer}"), 1)
                do(tt(rk, rk, sl, ALU.mult))
                do(dv.tensor_scalar(rk, rk, -1.0, None, ALU.add))
                do(dv.memset(nch[1], 1.0))
                for c in range(1, ntok // CAP):
                    do(dv.tensor_scalar(nch[2], nch[0], float(c * CAP), None, ALU.is_gt))
                    do(tt(nch[1], nch[1], nch[2], ALU.add))
                do(dv.memset(nch[0], 1.0))
                do(dv.tensor_tensor_scan(nch[2], nch[0], nch[1], 0.0, ALU.mult, ALU.add))
                do(dv.memset(cum[:, 0:1], 0))
                past = v3(h_t, 0, CHUNKS, NE)
                do(tt(past, nch[2].unsqueeze(1).broadcast_to([P, CHUNKS, NE]),
                      cn("iota", 0, CHUNKS).unsqueeze(2).broadcast_to([P, CHUNKS, NE]), ALU.is_le))
                do(dv.tensor_reduce(per_chunk, past, AX, ALU.add))
                do(dv.tensor_scalar(owner[:, :], per_chunk, NE - 1.0, None, ALU.min))
                do(tt(past, past, nch[1].unsqueeze(1).broadcast_to([P, CHUNKS, NE]), ALU.mult))
                do(dv.tensor_reduce(per_chunk, past, AX, ALU.add))
                do(tt(per_chunk, cn("iota", 0, CHUNKS), per_chunk, ALU.subtract))
                do(dv.tensor_scalar(per_chunk, per_chunk, float(CAP), None, ALU.mult))
                do(dv.memset(acc[:, :, 0:ntok], 0.0))
                dv.tensor_copy(cum[:, 1:NE + 1], nch[2]).then_inc(sem(f"table_ready{layer}"), 1)
                dv.wait_ge(sem(f"table_ready{layer}"), 1)

                s = {k: sem(f"{k}{layer}") for k in ("rows_full", "placed", "dispatch_ready", "combine_ready", "gt_full",
                                                      "gate_weights", "gt_taken", "gate_taken", "up_full", "hid_ready",
                                                      "hi_ready", "lo_ready", "y_full", "part_full", "part_added")}
                dv.sem_inc(s["hid_ready"], 1)

                def place_tokens(n):
                    e = dv.value_load(owner[0:1, bass.ds(n, 1)], min_val=0, max_val=NE - 1)
                    dv.wait_ge(s["rows_full"], n * 2 + 2)
                    dv.tensor_scalar(place[:, 0:tiles], rank[:, 0:tiles, bass.ds(e, 1)].rearrange("p t o -> p (t o)"),
                                     per_chunk[:, bass.ds(n, 1)], None, ALU.subtract).then_inc(s["placed"], 1)
                    dv.wait_ge(s["placed"], n + 1)
                    tt(disp[:, 0:tiles, :], cn("iota", 0, CAP).unsqueeze(1).broadcast_to([P, tiles, CAP]),
                       place[:, 0:tiles].unsqueeze(2).broadcast_to([P, tiles, CAP]), ALU.is_equal) \
                        .then_inc(s["dispatch_ready"], 1)
                    return e

                def weigh_tokens(n, e):
                    dv.wait_ge(s["dispatch_ready"], n + 1)
                    dv.wait_ge(s["gt_full"], n + 1)
                    tt(comb[:, 0:tiles, :], disp_f[:, 0:tiles, :],
                       gates[:, 0:tiles, bass.ds(e, 1)].broadcast_to([P, tiles, CAP]), ALU.mult) \
                        .then_inc(s["combine_ready"], 1)

                weigh_tokens(0, place_tokens(0))
                dv.sem_inc(s["part_added"], KD)
                total = dv.value_load(cum[0:1, NE:NE + 1], min_val=1, max_val=MOST)
                with dv.Fori(0, total) as n:
                    e = place_tokens(n + 1)
                    dv.wait_ge(s["gate_taken"], n + 1)
                    dv.wait_ge(s["up_full"], n + 1)
                    tt(hid.rearrange("p m s -> p (m s)"), silu_g, bank[2][:, :], ALU.mult).then_inc(s["hid_ready"], 1)
                    dv.wait_ge(s["gt_full"], n + 2)
                    dv.tensor_reduce(slot_gate, bank[3][:, 0:ntok], AX, ALU.add).then_inc(s["gate_weights"], 1)
                    dv.tensor_scalar(comb_t[:, 0:ntok], bank[3][:, 0:ntok], 0.0, None, ALU.is_gt) \
                        .then_inc(s["gt_taken"], 1)
                    weigh_tokens(n + 1, e)
                    dv.wait_ge(s["gate_weights"], n + 1)
                    for half in range(2):
                        dv.wait_ge(s["hi_ready"], n * 2 + half + 1)
                        cols = slice(half * 512, (half + 1) * 512)
                        dv.scalar_tensor_tensor(y_lo[:, cols], bank[4 + half][:, :], slot_gate, y_hi_f[:, cols],
                                                ALU.mult, ALU.subtract).then_inc(s["lo_ready"], 1)
                    for k in range(KD):
                        dv.wait_ge(s["part_full"], n * KD + k + 1)
                        dv.wait_ge(s["part_added"], n * KD + k + 1)
                        tt(acc[:, k, 0:ntok], acc[:, k, 0:ntok], bank[PART_BANKS[k]][:, 0:ntok], ALU.add) \
                            .then_inc(s["part_added"], 1)
                dv.wait_ge(s["part_added"], total * KD + KD)
                dv.tensor_copy(small[:, 0:1], acc[:, 0, 0:1]).then_inc(sem(f"moe_done{layer}"), 1)

            def residual(y, ntok):
                do(dv.scalar_tensor_tensor(X[:, :, 0:ntok], X[:, :, 0:ntok], ALPHA, y[:, :, 0:ntok], ALU.mult, ALU.add))

            def block_norm(i, ntok):
                layer_norm(f"ln{i}", X[:, :, 0:ntok], KD, ntok, v3(b12, 4096, KD, TOK)[:, :, 0:ntok], f"x_hat{i}")
                dv.wait_ge(sem(f"x_normed{i}"), 1)

            dv.memset(ones_d[:, :], 1.0 / D).then_inc(sem("ones"), 1)
            dv.memset(ones_m[:, :], 1.0 / 512).then_inc(sem("ones"), 1)
            dv.memset(ones_c[:, :], 1.0).then_inc(sem("ones"), 1)
            dv.wait_ge(sem("params"), 16)
            dv.wait_ge(sem("consts"), 16)
            do(dv.memset(b3[:, :], 0.0))
            for k in range(0, KD, 2):
                b = full()
                taken(dv.tensor_copy(X[:, k, :], b[:, :]))
            modulation(0, "ada_b0")
            modulation(1, "ada_b1")
            modulation(2, "b_mod")
            dv.tensor_copy(st[:, 0:1], mods[:, 0:1]).then_inc(sem("mods_ready"), 1)
            dv.wait_ge(sem("mods_ready"), 1)
            dv.wait_ge(a_free, marks["mods"][1])
            modulate(0, 0, "h_v0")

            for m in range(4):
                b = full()
                taken(dv.tensor_copy(a_val[:, m, :], b[:, :]))
            done()
            for m in range(4):
                dv.wait_ge(a_free, marks["mods"][1] + m + 1)
                for s_ in range(2):
                    step(tt(ya_pad[:, m, s_, PAD:PAD + SEQ], a_val[:, m, s_ * SEQ:(s_ + 1) * SEQ],
                            a_sig[:, m, s_ * SEQ:(s_ + 1) * SEQ], ALU.mult))
            done()
            for tap in range(TAPS):
                for m in range(4):
                    o = a_val[:, m, :].rearrange("p (s n) -> p s n", s=2)
                    src = ya_pad[:, m, :, tap:tap + SEQ]
                    wt = pr("dwa", m * TAPS + tap, 1)
                    if tap == 0:
                        step(dv.tensor_scalar(o, src, wt, pr("dw_b", m, 1), ALU.mult, ALU.add))
                    else:
                        dv.wait_ge(step.sem, step.n - 3)
                        step(dv.scalar_tensor_tensor(o, src, wt, o, ALU.mult, ALU.add))
            for m in range(4):
                b = full()
                dv.wait_ge(a_free, marks["mods"][1] + 8 + m + 1)
                for s_ in range(2):
                    ins = tt(cb_pad[:, m, s_, 1:1 + SEQ], b[:, s_ * SEQ:(s_ + 1) * SEQ],
                             c_gate[:, m, s_ * SEQ:(s_ + 1) * SEQ], ALU.mult)
                    (taken if s_ else step)(ins)
            done()
            for tap in range(3):
                for m in range(4):
                    o = a_sig[:, m, :].rearrange("p (s n) -> p s n", s=2)
                    src = cb_pad[:, m, :, tap:tap + SEQ]
                    wt = pr("dwb", m * 3 + tap, 1)
                    if tap == 0:
                        step(dv.tensor_scalar(o, src, wt, None, ALU.mult))
                    else:
                        dv.wait_ge(step.sem, step.n - 3)
                        step(dv.scalar_tensor_tensor(o, src, wt, o, ALU.mult, ALU.add))
            done()
            tt(a_sig, a_sig, b_gate, ALU.mult).then_inc(sem("conv_yb"), 1)
            layer_norm("cln", a_val, 4, TOK, v3(b3, 0, 4, TOK), "ya_hat")
            dv.wait_ge(a_free, marks["y_conv"][1])
            residual(H, TOK)
            block_norm(0, TOK)
            modulate(0, 3, "h2_v0")
            moe(0, 4)
            dv.wait_ge(sem("y_moe0"), 1)
            residual(H, TOK)
            block_norm(1, TOK)
            modulate(1, 0, "h_v1")

            for t in range(2):
                b = full()
                taken(dv.tensor_copy(q_tok[:, t, :], b[:, :]))
            for t in range(4):
                b = full()
                taken(dv.tensor_copy(kv_tok[:, t, :], b[:, 0:256]))
            done()
            sq = b3[:, 1024:2048]
            tab = lambda name, t: v3(con, CONST_AT[name][0] + 32 * t, 2, 16)
            rot = b3[:, 2048:3072]
            for name, rows_, nh, ntile, g_name in (("q", q_tok, 8, 2, "q_g"), ("k", kv_tok, 2, 4, "k_g")):
                for t in range(ntile):
                    z = rows_[:, t, 0:nh * HD].rearrange("p (h d) -> p h d", h=nh)
                    s_ = v3(b3, 1024, nh, HD)
                    root, inv = st[:, 16:16 + nh], st[:, 32:32 + nh]
                    do(tt(s_, z, z, ALU.mult))
                    do(dv.tensor_reduce(st[:, 0:nh], s_, AX, ALU.add))
                    idx = (0 if name == "q" else 2) + t + 1
                    dv.tensor_scalar(st[:, 0:nh], st[:, 0:nh], 1.0 / HD, RMS_EPS, ALU.mult, ALU.add) \
                        .then_inc(sem("head_var"), 1)
                    dv.wait_ge(sem("head_root"), idx)
                    do(dv.reciprocal(inv, root))
                    do(tt(z, z, inv.unsqueeze(2).broadcast_to([P, nh, HD]), ALU.mult))
                    do(tt(z, z, pr(g_name).unsqueeze(1).broadcast_to([P, nh, HD]), ALU.mult))
                    if t < 2:
                        zz = rows_[:, t, 0:nh * HD].rearrange("p (h a f) -> p h a f", h=nh, a=4)
                        r_ = rot[:, 0:nh * HD].rearrange("p (h a f) -> p h a f", h=nh, a=4)
                        for ax in range(2):
                            c = tab("cos", t)[:, ax, :].unsqueeze(1).broadcast_to([P, nh, 16])
                            s2 = tab("sin", t)[:, ax, :].unsqueeze(1).broadcast_to([P, nh, 16])
                            x1, x2 = zz[:, :, 2 * ax, :], zz[:, :, 2 * ax + 1, :]
                            a1, a2 = r_[:, :, 2 * ax, :], r_[:, :, 2 * ax + 1, :]
                            step(tt(a1, x2, s2, ALU.mult))
                            step(tt(a2, x1, s2, ALU.mult))
                            done()
                            step(tt(x1, x1, c, ALU.mult))
                            step(tt(x2, x2, c, ALU.mult))
                            done()
                            step(tt(x1, x1, a1, ALU.subtract))
                            step(tt(x2, x2, a2, ALU.add))
                        done()
            for t in range(4):
                for j in range(2):
                    for half in range(2):
                        ins = dv.tensor_copy(kdup[:, t, j, half * HD:(half + 1) * HD], kv_tok[:, t, j * HD:(j + 1) * HD])
            ins.then_inc(sem("rope_done"), 1)
            for j in range(4):
                b = full()
                taken(dv.tensor_copy(qc_t[:, j, :], b[:, 0:SEQ]))
            for j in range(2):
                b = full()
                taken(dv.tensor_copy(kc_t[:, j, :], b[:, :]))
            done()
            stat = lambda i, u: st[:, 64 + 2 * i + u % 2:65 + 2 * i + u % 2]

            def soften(u):
                kind, h, t = u // 16, (u % 16) // 2, u % 2
                dv.wait_ge(sem("score_full"), u + 1)
                if u >= 2:
                    dv.wait_ge(sem("exp_done"), u - 1)
                b = bank[u % 2]
                if kind == 0:
                    do(dv.tensor_reduce(stat(0, u), b[:, :], AX, ALU.max))
                    dv.tensor_scalar(stat(1, u), stat(0, u), -SCALE, None, ALU.mult).then_inc(sem("shift_ready"), 1)
                else:
                    lg = logit[u % 2]
                    if t == 0:
                        dv.wait_ge(sem(f"bias_in{h % 2}"), 64 * (h // 2 + 1))
                        bi = bias[h % 2].rearrange("p t (r c) -> p t r c", r=4)
                        for tt_ in range(2):
                            step(tt(bi[:, tt_], bi[:, tt_], cn("window").unsqueeze(1).broadcast_to([P, 4, 64]), ALU.add))
                        done()
                    step(dv.scalar_tensor_tensor(lg[:, 0:SEQ], b[:, 0:SEQ], SCALE, bias[h % 2][:, t, :], ALU.mult, ALU.add))
                    step(dv.tensor_scalar(lg[:, SEQ:TOK], b[:, SEQ:TOK], SCALE, None, ALU.mult))
                    done()
                    do(dv.tensor_reduce(stat(0, u), lg, AX, ALU.max))
                    dv.tensor_scalar(stat(1, u), stat(0, u), -1.0, None, ALU.mult).then_inc(sem("shift_ready"), 1)

            def gather(u):
                kind, h, t = u // 16, (u % 16) // 2, u % 2
                dv.wait_ge(sem("exp_done"), u + 1)
                if u:
                    dv.wait_ge(sem("o_taken"), u)
                do(dv.reciprocal(st[:, 96:97], stat(2, u)))
                dv.wait_ge(sem("o_full"), u + 1)
                c = 512 * kind + HD * h
                dv.tensor_scalar(o_tok[:, t, c:c + HD], bank[4 + u % 2][:, 0:HD], st[:, 96:97], None, ALU.mult) \
                    .then_inc(sem("o_taken"), 1)

            dv.wait_ge(a_free, marks["attention_in"][1])
            soften(0)
            for u in range(32):
                if u < 31:
                    soften(u + 1)
                gather(u)
            for k in range(0, KD, 2):
                b = full()
                taken(dv.tensor_copy(o_t[:, k, :], b[:, 0:SEQ]))
            dv.wait_ge(a_free, marks["y_attn"][1])
            residual(y_gated, SEQ)
            block_norm(2, SEQ)
            modulate(1, 3, "h2_v1")
            moe(1, 2)
            dv.wait_ge(sem("y_moe1"), 1)
            residual(H, SEQ)
            block_norm(3, SEQ)

            def rms(name, gain, i_scale, i_shift):
                s = [x[:, 0:SEQ] for x in ln_s]
                big = v3(b12, 4096, KD, SEQ)
                do(tt(big, X2, X2, ALU.mult))
                k_sum(s[0], big, SEQ).then_inc(sem(f"{name}_sum0"), 1)
                if name == "rms3":
                    dv.wait_ge(sem("rms3_full"), 1)
                    dv.tensor_scalar(s[1], bank[0][:, 0:SEQ], RMS_EPS, None, ALU.add).then_inc(sem("rms3_var"), 1)
                else:
                    b = full()
                    taken(dv.tensor_scalar(s[1], b[:, 0:SEQ], RMS_EPS, None, ALU.add))
                dv.wait_ge(sem(f"{name}_root"), 1)
                do(dv.reciprocal(s[1], s[2]))
                o = X2 if i_scale is None else U
                do(tt(o, X2, s[1].unsqueeze(1).broadcast_to([P, KD, SEQ]), ALU.mult))
                for k in range(KD):
                    if i_scale is None:
                        ins = dv.tensor_scalar(o[:, k, :], o[:, k, :], pr(gain, k, 1), None, ALU.mult)
                    else:
                        do(tt(st[:, k:k + 1], pr(gain, k, 1), mod(2, i_scale, k, 0), ALU.mult))
                        ins = dv.tensor_scalar(o[:, k, :], o[:, k, :], st[:, k:k + 1], mod(2, i_shift, k, 0),
                                               ALU.mult, ALU.add)
                    if k < KD - 1:
                        step(ins)
                return ins

            rms("rms1", "norm1", 1, 0).then_inc(sem("u1_ready"), 1)
            dv.wait_ge(sem("u1_ready"), 1)

            c16 = [st[:, 100 + 16 * i:116 + 16 * i] for i in range(14)]
            dt, mag, frac, cosv, sinv, den, k_re, k_im, ta, tb, lre, lim, turn, _ = c16
            dv.wait_ge(sem("dt_ready"), 1)
            do(tt(ta, pr("a_re"), dt, ALU.mult))
            do(tt(tb, pr("a_im"), dt, ALU.mult))
            do(dv.tensor_scalar(turn, tb, 1.0 / (2 * np.pi), None, ALU.mult))

            def wrap(o, a, tmp_):
                do(dv.tensor_scalar(tmp_, a, ROUND, None, ALU.add))
                do(dv.tensor_scalar(tmp_, tmp_, ROUND, None, ALU.subtract))
                do(tt(o, a, tmp_, ALU.subtract))

            wrap(turn, turn, frac)
            do(dv.tensor_scalar(cosv, turn, 0.25, None, ALU.add))
            do(dv.tensor_scalar(frac, cosv, ROUND, None, ALU.add))
            do(dv.tensor_scalar(frac, frac, ROUND, None, ALU.subtract))
            tt(cosv, cosv, frac, ALU.subtract).then_inc(sem("angle_ready"), 1)
            dv.wait_ge(sem("angle_done"), 3)
            do(tt(lre, mag, cosv, ALU.mult))
            do(tt(lim, mag, sinv, ALU.mult))
            do(dv.tensor_scalar(lre, lre, -1.0, None, ALU.add))
            do(tt(den, pr("a_re"), pr("a_re"), ALU.mult))
            do(tt(ta, pr("a_im"), pr("a_im"), ALU.mult))
            do(tt(den, den, ta, ALU.add))
            do(dv.reciprocal(den, den))
            for o, x1, y1, x2, y2, op in ((k_re, lre, "a_re", lim, "a_im", ALU.add), (k_im, lim, "a_re", lre, "a_im", ALU.subtract)):
                do(tt(ta, x1, pr(y1), ALU.mult))
                do(tt(tb, x2, pr(y2), ALU.mult))
                do(tt(o, ta, tb, op))
                do(tt(o, o, den, ALU.mult))
            bre, bim = v3(par, PARAM_AT["b_re"][0], 16, 16), v3(par, PARAM_AT["b_im"][0], 16, 16)
            w16 = lambda a: a.unsqueeze(2).broadcast_to([P, 16, 16])
            ts = [v3(b12, 4096 + 256 * i, 16, 16) for i in range(4)]
            step(tt(ts[0], bre, w16(k_re), ALU.mult))
            step(tt(ts[1], bim, w16(k_im), ALU.mult))
            step(tt(ts[2], bim, w16(k_re), ALU.mult))
            step(tt(ts[3], bre, w16(k_im), ALU.mult))
            done()
            step(tt(bre, ts[0], ts[1], ALU.subtract))
            step(tt(bim, ts[2], ts[3], ALU.add))
            done()
            expand = Count(sem("s5_expanded"))
            for i in range(16):
                kind, ci = i // 4, i % 4
                if i >= 4:
                    b = full()
                    taken(dv.tensor_copy(s5w(i - 4), b[:, 0:P]))
                e = expanded(i)
                if kind < 2:
                    src = (bre, bim)[kind]
                    do(dv.memset(e, 0.0))
                    ev = e.rearrange("p (j g c) -> p j g c", j=4, g=2)
                    step(dv.tensor_copy(ev[0:64, :, 0, :], src[0:64, 4 * ci:4 * ci + 4, :]))
                    expand(dv.tensor_copy(ev[64:128, :, 1, :], src[64:128, 4 * ci:4 * ci + 4, :]))
                else:
                    src = pr("c_re" if kind == 2 else "c_im", 64 * ci, 64)
                    step(dv.tensor_scalar(e[:, 0:64], src, cn("parity", 0, 1), 1.0 if kind == 2 else -1.0, ALU.mult, ALU.mult))
                    expand(dv.tensor_scalar(e[:, 64:128], src, cn("parity", 1, 1), 1.0 if kind == 2 else -1.0,
                                            ALU.mult, ALU.mult))
            for i in range(12, 16):
                b = full()
                taken(dv.tensor_copy(s5w(i), b[:, 0:P]))
            for m in range(4):
                b = full()
                taken(dv.tensor_copy(xs_t[:, m, :], b[:, 0:SEQ]))
            for t in range(2):
                b = full()
                taken(dv.tensor_copy(misc[:, t, :], b[:, 0:452]))
            dv.wait_ge(a_free, marks["in_proj"][1])
            done()
            scan = Count(sem("scan_done"))
            for i in range(4):
                it = cn("iota").unsqueeze(1).broadcast_to([P, 4, SEQ])
                th = turn[:, 4 * i:4 * i + 4].unsqueeze(2).broadcast_to([P, 4, SEQ])
                do(tt(t_a, it, th, ALU.mult))
                wrap(sin_t, t_a, t_b)
                do(dv.tensor_scalar(cos_t, sin_t, 0.25, None, ALU.add))
                do(dv.tensor_scalar(t_b, cos_t, ROUND, None, ALU.add))
                do(dv.tensor_scalar(t_b, t_b, ROUND, None, ALU.subtract))
                tt(cos_t, cos_t, t_b, ALU.subtract).then_inc(sem("phase_ready"), 1)
                for u_ in (u_re, u_im):
                    for jj in range(4):
                        b = full()
                        taken(dv.tensor_copy(u_[:, jj, :], b[:, 0:SEQ]))
                dv.wait_ge(sem("phase_done"), 2 * (i + 1))
                done()
                step(tt(z_re, u_re, cos_t, ALU.mult))
                step(tt(t_a, u_im, sin_t, ALU.mult))
                step(tt(z_im, u_im, cos_t, ALU.mult))
                step(tt(t_b, u_re, sin_t, ALU.mult))
                done()
                step(tt(z_re, z_re, t_a, ALU.add))
                step(tt(z_im, z_im, t_b, ALU.subtract))
                done()
                for jj in range(4):
                    m_ = mag[:, 4 * i + jj:4 * i + jj + 1].broadcast_to([P, SEQ])
                    step(dv.tensor_tensor_scan(u_re[:, jj, :], m_, z_re[:, jj, :], 0.0, ALU.mult, ALU.add))
                    step(dv.tensor_tensor_scan(u_im[:, jj, :], m_, z_im[:, jj, :], 0.0, ALU.mult, ALU.add))
                done()
                step(tt(z_re, u_re, cos_t, ALU.mult))
                step(tt(t_a, u_im, sin_t, ALU.mult))
                step(tt(z_im, u_im, cos_t, ALU.mult))
                step(tt(t_b, u_re, sin_t, ALU.mult))
                done()
                do(tt(z_re, z_re, t_a, ALU.subtract))
                scan(tt(z_im, z_im, t_b, ALU.add))
                b = full()
                taken(dv.scalar_tensor_tensor(y_ssm[:, i, :], xs_t[:, i, :], pr("ssm_d", i, 1), b[:, 0:SEQ],
                                              ALU.mult, ALU.add))
                done()
            do(tt(z_re, y_ssm, y_ssm, ALU.mult))
            do(dv.tensor_scalar(z_re, z_re, 0.044715, 1.0, ALU.mult, ALU.add))
            tt(z_re, z_re, y_ssm, ALU.mult).then_inc(sem("gelu_arg"), 1)
            dv.wait_ge(sem("gelu_tanh"), 1)
            do(dv.tensor_scalar(z_im, z_im, 0.5, 0.5, ALU.mult, ALU.add))
            tt(y_ssm, y_ssm, z_im, ALU.mult).then_inc(sem("y_gelu"), 1)
            dv.wait_ge(a_free, marks["glu"][1])
            do(tt(val, val, sig, ALU.mult))
            do(tt(sga, sga, val, ALU.mult))

            for t in range(2):
                for lo, n_, g_name, idx in ((0, 128, "kv_g", 2 * t), (384, 64, "ki_g", 2 * t + 1)):
                    z = misc[:, t, lo:lo + n_]
                    do(tt(b3[:, 0:n_], z, z, ALU.mult))
                    do(dv.tensor_reduce(st[:, 0:1], b3[:, 0:n_], AX, ALU.add))
                    dv.tensor_scalar(st[:, 0:1], st[:, 0:1], 1.0 / n_, RMS_EPS, ALU.mult, ALU.add).then_inc(sem("kv_var"), 1)
                    dv.wait_ge(sem("kv_root"), idx + 1)
                    do(dv.reciprocal(st[:, 2:3], st[:, 1:2]))
                    do(dv.tensor_scalar(z, z, st[:, 2:3], None, ALU.mult))
                    do(tt(z, z, pr(g_name), ALU.mult))
                step(dv.tensor_copy(ki_dup[t][:, 0:64], misc[:, t, 384:448]))
                do(dv.tensor_copy(ki_dup[t][:, 64:128], misc[:, t, 384:448]))
                do(dv.tensor_scalar(st[:, 4 + 4 * t:8 + 4 * t], misc[:, t, 448:452], 0.5, None, ALU.mult))
            dv.tensor_copy(st[:, 0:1], st[:, 2:3]).then_inc(sem("dsa_norm"), 1)
            for t in range(2):
                for o in (ckv_t[:, t * P:(t + 1) * P], ki_t[:, t * P:(t + 1) * P],
                          qi_t[:, 0, t * P:(t + 1) * P], qi_t[:, 1, t * P:(t + 1) * P]):
                    b = full()
                    taken(dv.tensor_copy(o, b[:, 0:P]))
            for j in range(4):
                b = full()
                taken(dv.tensor_copy(wuk_t[:, j, :], b[:, 0:P]))
            dv.wait_ge(sem("dsa_norm"), 1)
            done()
            for t in range(2):
                dv.wait_ge(a_free, marks["glu"][1] + 4 * (t + 1))
                c = v3(con, CONST_AT["causal"][0], 2, SEQ)[:, t, :]
                do(dv.tensor_scalar(isc, relu4[t][:, 0, :], st[:, 4 + 4 * t:5 + 4 * t], None, ALU.mult))
                for hh in range(1, 4):
                    do(dv.scalar_tensor_tensor(isc, relu4[t][:, hh, :], st[:, 4 + 4 * t + hh:5 + 4 * t + hh], isc,
                                               ALU.mult, ALU.add))
                do(tt(isc, isc, c, ALU.mult))
                do(dv.tensor_scalar(ties, c, -1.0, -LOW, ALU.add, ALU.mult))
                do(tt(isc, isc, ties, ALU.add))
                src = isc
                for r in range(TOPK // 8):
                    do(dv.max(st[:, 16:24], src))
                    if r < TOPK // 8 - 1:
                        do(dv.match_replace(work, st[:, 16:24], src, LOW))
                        src = work
                thr = st[:, 23:24]
                do(dv.tensor_scalar(work, isc, thr, None, ALU.is_gt))
                do(dv.tensor_reduce(st[:, 24:25], work, AX, ALU.add))
                do(dv.tensor_scalar(st[:, 24:25], st[:, 24:25], -1.0, float(TOPK), ALU.mult, ALU.add))
                do(dv.tensor_scalar(ties, isc, thr, None, ALU.is_equal))
                do(dv.memset(relu, 1.0))
                do(dv.tensor_tensor_scan(mask[:, t, :], relu, ties, 0.0, ALU.mult, ALU.add))
                do(dv.tensor_scalar(mask[:, t, :], mask[:, t, :], st[:, 24:25], None, ALU.is_le))
                do(tt(mask[:, t, :], mask[:, t, :], ties, ALU.mult))
                do(tt(mask[:, t, :], mask[:, t, :], work, ALU.add))
                do(tt(mask[:, t, :], mask[:, t, :], c, ALU.mult))
                do(dv.tensor_scalar(mask[:, t, :], mask[:, t, :], -1.0, -NEG, ALU.add, ALU.mult))
            for h in range(HEADS):
                b = full()
                taken(dv.tensor_scalar(q_lat[h % 2], b[:, 0:SEQ], SCALE, None, ALU.mult))
                for t in range(2):
                    u = 2 * h + t
                    b = full()
                    taken(tt(p2[t], b[:, 0:SEQ], mask[:, t, :], ALU.add))
                    done()
                    do(dv.tensor_reduce(st[:, 32:33], p2[t], AX, ALU.max))
                    dv.tensor_scalar(st[:, 33:34], st[:, 32:33], -1.0, None, ALU.mult).then_inc(sem("shift2_ready"), 1)
                    dv.wait_ge(sem("exp2_done"), u + 1)
                    do(dv.reciprocal(st[:, 35:36], st[:, 34:35]))
                    dv.tensor_scalar(p2[t], p2[t], st[:, 35:36], None, ALU.mult).then_inc(sem("p2_ready"), 1)
                    b = full()
                    if h >= 2 and t == 0:
                        dv.wait_ge(a_free, marks["heads"][1] + 3 * (h - 1))
                    taken(dv.tensor_copy(lat_o[h % 2][:, t * P:(t + 1) * P], b[:, 0:P]))
            for m in range(KD):
                b = full()
                taken(tt(sgb[:, m, :], sgb[:, m, :], b[:, 0:SEQ], ALU.mult))
            done()
            tt(sga, sga, sgb, ALU.add).then_inc(sem("merged"), 1)
            dv.wait_ge(a_free, marks["y_block2"][1])
            do(tt(X2, X2, U, ALU.add))
            rms("rms2", "norm2", 4, 3).then_inc(sem("u2_ready"), 1)
            for m in range(KF):
                b = full()
                dv.wait_ge(a_free, marks["ffn"][1] + m + 1)
                taken(tt(f_hid[:, m, :], f_sil[:, m % 4, :], b[:, 0:SEQ], ALU.mult))
            dv.wait_ge(sem("y_ffn"), 1)
            dv.wait_ge(sem("u2_ready"), 1)
            do(tt(X2, X2, U, ALU.add))
            rms("rms3", "final", None, None).then_inc(sem("final_ready"), 1)
            for t in range(2):
                dv.wait_ge(sem("final_full"), 2 * t + 1)
                dv.tensor_copy(fin[:, t, 0:512], bank[1 + 2 * t][:, :]).then_inc(sem("fin_v"), 1)

        @block.scalar
        def _(ac):
            taken = Count(a_free)

            def full():
                ac.wait_ge(a_full, taken.n + 1)
                return A_BANKS[taken.n % 4]

            def act(o, i, f, **kw):
                return ac.activation(o, i, f, **kw)

            def modulate(i, part, event):
                for k in range(KD):
                    ins = act(H[:, k, SEQ:TOK], X[:, k, SEQ:TOK], ACT.Identity, scale=mod(i, part + 1, k, 1),
                              bias=mod(i, part, k, 1))
                ins.then_inc(sem(event), 1)

            def root(name, ntok):
                if name == "rms3":
                    ac.wait_ge(sem("rms3_var"), 1)
                else:
                    ac.wait_ge(v_free, marks[name][0])
                act(ln_s[2][:, 0:ntok], ln_s[1][:, 0:ntok], ACT.Sqrt).then_inc(sem(f"{name}_root"), 1)

            def gain(i, j, ntok, g_name, b_name):
                root(f"ln{i}", ntok)
                ac.wait_ge(sem(f"x_hat{i}"), 1)
                for k in range(KD):
                    ins = act(X[:, k, 0:ntok], X[:, k, 0:ntok], ACT.Identity, scale=pr(g_name, 8 * j + k, 1),
                              bias=pr(b_name, 8 * j + k, 1))
                ins.then_inc(sem(f"x_normed{i}"), 1)
                ac.wait_ge(sem(f"x_normed{i}"), 1)

            def gated(i, part, ntok, o):
                for m in range(KD):
                    b = full()
                    for src in range(ntok // SEQ):
                        ins = act(o[:, m, src * SEQ:(src + 1) * SEQ], b[:, src * SEQ:(src + 1) * SEQ], ACT.Copy,
                                  scale=mod(i, part, m, src))
                    taken(ins)

            def moe(layer, tiles):
                ntok = tiles * P
                copied = Count(sem(f"h_copied{layer}"))

                def copy_h(i):
                    b, t, cols = full(), i // 2, slice(i % 2 * 512, (i % 2 + 1) * 512)
                    copied(act(h_hi[:, t, cols], b[:, :], ACT.Copy))
                    taken(act(h_lo_full[:, t, cols], b[:, :], ACT.Copy))

                for i in range(2 * tiles):
                    copy_h(i)
                g = [small[:, 4 * i:4 * i + tiles] for i in range(8)]
                four = [v3(small, 32 + 16 * i, 4, NG)[:, 0:tiles, :] for i in range(3)]
                ac.wait_ge(sem(f"group_shift{layer}"), 1)
                act(four[2], four[1], ACT.Exp).then_inc(sem(f"group_exp{layer}"), 1)
                ac.wait_ge(sem(f"pair_shift{layer}"), 1)
                act(g[5], g[4], ACT.Exp).then_inc(sem(f"pair_exp{layer}"), 1)
                s = {k: sem(f"{k}{layer}") for k in ("rows_full", "rows_taken", "xe_full", "xe_taken", "gate_full",
                                                      "gate_taken", "gate_weights", "y_full", "hi_ready", "hid_ready")}
                ac.sem_inc(s["xe_taken"], 1)
                ac.wait_ge(sem(f"table_ready{layer}"), 1)
                total = ac.value_load(cum[0:1, NE:NE + 1], min_val=1, max_val=MOST)

                def take_rows(n):
                    for half in range(2):
                        ac.wait_ge(s["rows_full"], n * 2 + half + 3)
                        ins = act(xe_rows[:, half * 512:(half + 1) * 512], bank[half][:, :], ACT.Copy)
                    ins.then_inc(s["rows_taken"], 1)

                def take_xe(n):
                    ac.wait_ge(s["xe_full"], n + 1)
                    for half in range(2):
                        ins = act(xe[:, 4 * half:4 * half + 4, :].rearrange("p k s -> p (k s)"), bank[half][:, :], ACT.Copy)
                    ins.then_inc(s["xe_taken"], 1)

                take_rows(0)
                take_xe(0)
                with ac.Fori(0, total) as n:
                    ac.wait_ge(s["gate_full"], n + 1)
                    ac.wait_ge(s["hid_ready"], n + 1)
                    act(silu_g, bank[3][:, :], ACT.Silu).then_inc(s["gate_taken"], 1)
                    take_rows(n + 1)
                    take_xe(n + 1)
                    ac.wait_ge(s["gate_weights"], n + 1)
                    for half in range(2):
                        ac.wait_ge(s["y_full"], n * 2 + half + 1)
                        act(y_hi[:, half * 512:(half + 1) * 512], bank[4 + half][:, :], ACT.Copy, scale=slot_gate) \
                            .then_inc(s["hi_ready"], 1)
                ac.wait_ge(sem(f"moe_done{layer}"), 1)
                for k in range(KD):
                    for src in range(ntok // SEQ):
                        ins = act(H[:, k, src * SEQ:(src + 1) * SEQ], acc[:, k, src * SEQ:(src + 1) * SEQ], ACT.Copy,
                                  scale=mod(layer, 5, k, src))
                ins.then_inc(sem(f"y_moe{layer}"), 1)

            ac.dma_start(par[:, :], w["params"]).then_inc(sem("params"), 16)
            ac.dma_start(con[:, :], w["consts"]).then_inc(sem("consts"), 16)
            ac.wait_ge(sem("params"), 16)
            act(sm[:, 0:16], pr("cond"), ACT.Silu).then_inc(sem("cond_ready"), 1)
            act(cond2_s, pr("cond2"), ACT.Silu).then_inc(sem("cond_ready"), 1)
            for k in range(1, KD, 2):
                b = full()
                taken(act(X[:, k, :], b[:, :], ACT.Copy))
            for width in (2, 2, 1):
                for j in range(1, 12, 2):
                    b = full()
                    taken(act(mod_rows[0:width, j * 512:(j + 1) * 512], b[0:width, :], ACT.Copy))
            ac.wait_ge(sem("mods_ready"), 1)
            ac.wait_ge(v_free, 4)
            ac.wait_ge(a_free, taken.n)
            modulate(0, 0, "h_a0")
            for dst, f in ((a_sig, ACT.Sigmoid), (b_gate, ACT.Copy), (c_gate, ACT.Copy)):
                for m in range(4):
                    b = full()
                    taken(act(dst[:, m, :], b[:, :], f))
            root("cln", TOK)
            ac.wait_ge(sem("ya_hat"), 1)
            for m in range(4):
                ins = act(a_val[:, m, :], a_val[:, m, :], ACT.Silu, scale=pr("cln_g", m, 1), bias=pr("cln_b", m, 1))
            ins.then_inc(sem("conv_ya"), 1)
            gated(0, 2, TOK, H)
            gain(0, 0, TOK, "ln1_g", "ln1_b")
            modulate(0, 3, "h2_a0")
            moe(0, 4)
            gain(1, 0, TOK, "ln2_g", "ln2_b")
            modulate(1, 0, "h_a1")
            for m in range(4):
                b = full()
                taken(act(qd_t[:, m, :], b[:, 0:SEQ], ACT.Copy))
            for m in range(4):
                b = full()
                taken(act(kd_t[:, m, :], b[:, :], ACT.Copy))
            for t in range(4):
                b = full()
                taken(act(vd_tok[:, t, :], b[:, :], ACT.Copy))
            for i in range(6):
                nh = 8 if i < 2 else 2
                ac.wait_ge(sem("head_var"), i + 1)
                act(st[:, 16:16 + nh], st[:, 0:nh], ACT.Sqrt).then_inc(sem("head_root"), 1)

            def load_bias(h):
                for t in range(2):
                    for rr in range(2):
                        r0 = 3 - (2 * t + rr)
                        src = w["row_bias"][h, :, r0:r0 + 4, :]
                        ac.dma_start(bias[h % 2][64 * rr:64 * rr + 64, t, :].rearrange("p (r c) -> p r c", r=4), src) \
                            .then_inc(sem(f"bias_in{h % 2}"), 16)

            ac.wait_ge(sem("rope_done"), 1)
            load_bias(0)
            for u in range(32):
                kind, h, t = u // 16, (u % 16) // 2, u % 2
                i = u % 2
                if kind == 1 and t == 0 and h < 7:
                    if h >= 1:
                        ac.wait_ge(sem("shift_ready"), u)
                    load_bias(h + 1)
                ac.wait_ge(sem("shift_ready"), u + 1)
                if u >= 2:
                    ac.wait_ge(sem("pt_full"), u - 1)
                    ac.wait_ge(sem("o_taken"), u - 1)
                src = bank[u % 2][:, :] if kind == 0 else logit[i]
                act(prob[i], src, ACT.Exp, scale=SCALE if kind == 0 else 1.0, bias=st[:, 66 + i:67 + i],
                    accum_out=st[:, 68 + i:69 + i]).then_inc(sem("exp_done"), 1)
                ac.wait_ge(sem("pt_full"), u + 1)
                if u >= 2:
                    ac.wait_ge(sem("o_full"), u - 1)
                act(prob_t[i].rearrange("p k n -> p (k n)"), bank[2 + i][:, :], ACT.Copy).then_inc(sem("pt_taken"), 1)
            for k in range(1, KD, 2):
                b = full()
                taken(act(o_t[:, k, :], b[:, 0:SEQ], ACT.Copy))
            gated(1, 2, SEQ, y_gated)
            gain(2, 1, SEQ, "ln1_g", "ln1_b")
            moe(1, 2)
            gain(3, 1, SEQ, "ln2_g", "ln2_b")

            c16 = [st[:, 100 + 16 * i:116 + 16 * i] for i in range(14)]
            dt, mag, frac, cosv, sinv, den, k_re, k_im, ta, tb, lre, lim, turn, _ = c16
            act(dt, pr("log_dt"), ACT.Exp).then_inc(sem("dt_ready"), 1)
            root("rms1", SEQ)
            ac.wait_ge(sem("angle_ready"), 1)
            act(mag, ta, ACT.Exp).then_inc(sem("angle_done"), 1)
            act(sinv, turn, ACT.Sin, scale=TWO_PI).then_inc(sem("angle_done"), 1)
            act(cosv, cosv, ACT.Sin, scale=TWO_PI).then_inc(sem("angle_done"), 1)
            for m in range(4):
                b = full()
                taken(act(q2_t[:, m, :], b[:, 0:SEQ], ACT.Copy))
            for dst in (sga, sgb):
                for m in range(KD):
                    b = full()
                    taken(act(dst[:, m, :], b[:, 0:SEQ], ACT.Sigmoid))
            for i in range(4):
                ac.wait_ge(sem("phase_ready"), i + 1)
                act(sin_t, sin_t, ACT.Sin, scale=TWO_PI).then_inc(sem("phase_done"), 1)
                act(cos_t, cos_t, ACT.Sin, scale=TWO_PI).then_inc(sem("phase_done"), 1)
            ac.wait_ge(sem("gelu_arg"), 1)
            act(z_im, z_re, ACT.Tanh, scale=GELU_C).then_inc(sem("gelu_tanh"), 1)
            for m in range(KD):
                b = full()
                taken(act(val[:, m, :], b[:, 0:SEQ], ACT.Identity, bias=pr("b_glu", m, 1)))
            for m in range(KD):
                b = full()
                taken(act(sig[:, m, :], b[:, 0:SEQ], ACT.Sigmoid, bias=pr("b_glu", 8 + m, 1)))
            for i in range(4):
                ac.wait_ge(sem("kv_var"), i + 1)
                act(st[:, 1:2], st[:, 0:1], ACT.Sqrt).then_inc(sem("kv_root"), 1)
            for t in range(2):
                for hh in range(4):
                    b = full()
                    taken(act(relu4[t][:, hh, :], b[:, 0:SEQ], ACT.Relu, scale=SCALE))
            for h in range(HEADS):
                for t in range(2):
                    u = 2 * h + t
                    ac.wait_ge(sem("shift2_ready"), u + 1)
                    act(p2[t], p2[t], ACT.Exp, bias=st[:, 33:34], accum_out=st[:, 34:35]).then_inc(sem("exp2_done"), 1)
                    b = full()
                    taken(act(p2_t[t].rearrange("p k n -> p (k n)"), b[:, 0:SEQ], ACT.Copy))
                b = full()
                p0 = HD * (h % 2)
                taken(act(atto[p0:p0 + HD, h // 2, :], b[p0:p0 + HD, 0:SEQ], ACT.Copy))
            ac.wait_ge(sem("merged"), 1)
            gated(2, 2, SEQ, U)
            root("rms2", SEQ)
            for m in range(KF):
                b = full()
                if m >= 4:
                    ac.wait_ge(v_free, marks["ffn"][0] + m - 3)
                taken(act(f_sil[:, m % 4, :], b[:, 0:SEQ], ACT.Silu))
            ac.wait_ge(sem("u2_ready"), 1)
            for m in range(KD):
                ac.wait_ge(sem("down_full"), m + 1)
                ins = act(U[:, m, :], bank[m][:, 0:SEQ], ACT.Copy, scale=mod(2, 5, m, 0))
            ins.then_inc(sem("y_ffn"), 1)
            root("rms3", SEQ)
            for t in range(2):
                ac.wait_ge(sem("final_full"), 2 * t + 2)
                act(fin[:, t, 512:1024], bank[2 + 2 * t][:, :], ACT.Copy).then_inc(sem("fin_a"), 1)

        @block.sync
        def _(sp):
            x_rows = w["x"][0].rearrange("(t p) d -> p t d", p=P)
            c_rows = w["ctx"][0].rearrange("(t p) d -> p t d", p=P)
            for t in range(2):
                sp.dma_start(tok_in[:, t, :], x_rows[:, t, :]).then_inc(sem("x_in"), 16)
                sp.dma_start(tok_in[:, 2 + t, :], c_rows[:, t, :]).then_inc(sem("x_in"), 16)

            def load(n, src):
                sp.dma_start(chunk(n, src.shape[1], src.shape[2]), src).then_inc(slot_loaded[n % RING], 16)

            def straight(name, chunks, skip=0):
                for j, src in enumerate(chunks):
                    n = start[name] + j
                    if j >= skip and n >= RING:
                        v, a = read_by[n - RING]
                        sp.wait_ge(v_full, v)
                        if a:
                            sp.wait_ge(a_full, a)
                    load(n, src)

            def experts(layer):
                n0 = start[f"moe{layer}"]
                ws = [w["expert_w_gate"][layer].rearrange("e (k p) n -> e p k n", p=P),
                      w["expert_w_up"][layer].rearrange("e (k p) n -> e p k n", p=P),
                      w["expert_w_down"][layer].rearrange("e (k p) n -> e p k n", p=P)]
                for j in range(6):
                    v, a = read_by[n0 + j - RING]
                    sp.wait_ge(v_full, v)
                    if a:
                        sp.wait_ge(a_full, a)
                    load(n0 + j, ws[j % 3][j // 3])
                sp.wait_ge(sem(f"table_ready{layer}"), 1)
                y_full = sem(f"y_full{layer}")
                with sp.Fori(1, NE // 2) as pair:
                    for j in range(2):
                        done = sp.value_load(cum[0:1, bass.ds(pair * 2 + (j - 1), 1)], min_val=1, max_val=MOST)
                        sp.wait_ge(y_full, done * 2)
                        for i in range(3):
                            c = n0 + 3 * j + i
                            src = ws[i][bass.ds(pair * 2 + j, 1)].rearrange("e p k n -> (e p) k n")
                            sp.dma_start(chunk(c, src.shape[1], src.shape[2]), src).then_inc(slot_loaded[c % RING], 16)
                total = [sp.value_load(cum[0:1, i:i + 1], min_val=1, max_val=MOST) for i in (NE - 1, NE)]
                return total

            def after_experts(layer, name, chunks):
                total = experts(layer)
                for j in range(RING):
                    if j % 3 == 0:
                        sp.wait_ge(sem(f"y_full{layer}"), total[j // 3] * 2)
                    load(start[name] + j, chunks[j])
                straight_from(name, chunks, RING)

            def straight_from(name, chunks, first):
                for j in range(first, len(chunks)):
                    n = start[name] + j
                    v, a = read_by[n - RING]
                    sp.wait_ge(v_full, v)
                    if a:
                        sp.wait_ge(a_full, a)
                    load(n, chunks[j])

            straight("before", before)
            after_experts(0, "middle", middle)
            after_experts(1, "after", after)
            o = out[0].rearrange("(t p) d -> p t d", p=P)
            sp.wait_ge(sem("fin_v"), 2)
            sp.wait_ge(sem("fin_a"), 2)
            sp.dma_start(o, fin).then_inc(sem("stored"), 16)
            sp.wait_ge(sem("stored"), 16)


_WHOLE = ["x", "ctx", "ada_w", "w_mod_2", "conv_w_in", "conv_w_out", "attn_w_in", "attn_w_out",
          "expert_w_gate", "expert_w_up", "expert_w_down", "w_in_2", "w_ssm_glu_2", "w_attn_proj_2", "w_out_2",
          "w_ffn_gate_2", "w_ffn_up_2", "w_ffn_down_2"]


def packed_params(a):
    def cols(v):
        return v.reshape(-1, P).T

    def rows(v):
        return np.broadcast_to(v.reshape(1, -1), (P, v.size))

    def states(v):
        return v[0].reshape(STATES, P, *v.shape[3:]).swapaxes(0, 1).reshape(P, -1)

    def taps(v):
        return v[0].reshape(-1, 4, P).transpose(2, 1, 0).reshape(P, -1)

    def outs(v):
        return v[0].reshape(4, P, HD).swapaxes(0, 1).reshape(P, -1)

    parts = dict(
        cond=np.stack([cols(a["c"]), cols(a["c_ctx"])], 2).reshape(P, 16), cond2=cols(a["c_2"]),
        ada_b0=cols(a["ada_b"][0]), ada_b1=cols(a["ada_b"][1]), b_mod=cols(a["b_mod_2"]),
        ln1_g=cols(a["ln1_g"]), ln1_b=cols(a["ln1_b"]), ln2_g=cols(a["ln2_g"]), ln2_b=cols(a["ln2_b"]),
        dw_b=cols(a["conv_a_dw_b"]), cln_g=cols(a["conv_a_ln_g"]), cln_b=cols(a["conv_a_ln_b"]),
        dwa=taps(a["conv_a_dw_w"]), dwb=taps(a["conv_b_dw_w"]),
        norm1=cols(a["norm1_g_2"]), norm2=cols(a["norm2_g_2"]), final=cols(a["final_g_2"]),
        ssm_d=cols(a["ssm_d_2"]), b_glu=cols(a["b_ssm_glu_2"]),
        a_re=states(a["ssm_a_re_2"]), a_im=states(a["ssm_a_im_2"]),
        log_dt=np.repeat(a["ssm_log_dt_2"].reshape(STATES, 2).T, HD, 0),
        b_re=states(a["ssm_b_re_2"]), b_im=states(a["ssm_b_im_2"]),
        c_re=outs(a["ssm_c_re_2"]), c_im=outs(a["ssm_c_im_2"]),
        kv_g=rows(a["kv_norm_g_2"]), ki_g=rows(a["idx_k_norm_g_2"]), q_g=rows(a["q_norm_g"]), k_g=rows(a["k_norm_g"]),
        rb=rows(np.concatenate([a["router_b1"], a["router_b2"]], 1)),
        rw=np.concatenate([a["router_w1"], a["router_w2"]], 2).reshape(2, KD, P, 36).transpose(2, 0, 1, 3).reshape(P, -1),
        w_uk=a["w_uk_2"].reshape(P, -1), w_uv=a["w_uv_2"].reshape(P, -1))
    for name, width in PARAM.items():
        assert parts[name].shape == (P, width), name
    return np.ascontiguousarray(np.concatenate([parts[name] for name in PARAM], 1))


def packed_consts():
    p = np.arange(P)
    n = np.arange(SEQ)
    grid_w = 64
    f32 = np.float32
    inv = (f32(10000.0) ** (-np.arange(0, 32, 2, dtype=f32) / f32(32))).astype(f32)
    angle = np.stack([(n // grid_w).astype(f32)[:, None] * inv, (n % grid_w).astype(f32)[:, None] * inv], 1)
    tab = lambda f: f(angle).astype(f32).reshape(2, P, 32).swapaxes(0, 1).reshape(P, 64)
    qc, kc = p % grid_w, np.arange(grid_w)
    first = np.clip(qc - 8, 0, grid_w - 16)[:, None]
    parts = dict(
        ident=np.eye(P), before=p[:, None] < p[None, :], iota=np.broadcast_to(n, (P, SEQ)), cos=tab(np.cos), sin=tab(np.sin),
        window=np.where((kc >= first) & (kc < first + 16), 0.0, NEG),
        causal=(n[None, None, :] <= (p[:, None, None] + P * np.arange(2)[None, :, None])).reshape(P, 512),
        rev=np.broadcast_to(NE - np.arange(NE), (P, NE)), rev4=np.broadcast_to(NG - np.arange(NG), (P, NG)),
        parity=(p[:, None] // 16) % 2 == np.arange(2))
    return np.concatenate([np.asarray(parts[name], f32) for name in CONST], 1)


def kernel(**inputs):
    import concourse.bacc as bacc
    from concourse.bass_utils import run_bass_kernel_spmd

    a = {name: np.ascontiguousarray(v) for name, v in inputs.items()}
    nc = bacc.Bacc("TRN2", target_bir_lowering=False, num_devices=1)
    arrays = {name: a[name] for name in _WHOLE}
    arrays["params"] = packed_params(a)
    arrays["consts"] = packed_consts()
    col = np.clip(np.arange(64)[None, :] - np.arange(64)[:, None] + 15, 0, 30)
    arrays["row_bias"] = np.ascontiguousarray(a["na_rel_bias"][0][:, 4:11][:, :, col].transpose(0, 2, 1, 3))
    w = {name: nc.dram_tensor(f"in_{name}", v.shape, F32, kind="ExternalInput").ap() for name, v in arrays.items()}
    out = nc.dram_tensor("out_0", (1, SEQ, D), F32, kind="ExternalOutput").ap()
    two_blocks(nc, w, out)
    r = run_bass_kernel_spmd(nc, [{f"in_{name}": v for name, v in arrays.items()}], core_ids=[0])
    return r.results[0]["out_0"]
```
